# Optimizing a Trainium2 kernel written in Bass

```python
import math
import jax, jax.numpy as jnp
from jax import lax
import numpy as np

D_MODEL = 1024
BATCH = 1
SEQ = 1024
DEPTH = 1

HEAD_DIM = 64
D_MIX = D_MODEL
D_ATTN = D_MIX // 2
D_SGU = D_MIX - D_ATTN
N_ATTN_HEADS = D_ATTN // HEAD_DIM
N_SGU_GROUPS = D_SGU // HEAD_DIM
SGU_GROUP_DIM = D_SGU // N_SGU_GROUPS
D_IN_PROJ = 3 * D_ATTN + 2 * D_SGU
DILATED_BRANCHES = ((128, 1), (512, 4), (2048, 16))
SGU_CHUNK = 128
D_FF = 4 * D_MODEL
N_REL_BUCKETS = 32
REL_MAX_DISTANCE = 1024
RMS_EPS = 1e-6
LN_EPS = 1e-5
NEG_INF = -1e30


def rms_norm(x, g):
    xf = x.astype(jnp.float32)
    y = xf * lax.rsqrt(jnp.mean(xf * xf, axis=-1, keepdims=True) + RMS_EPS)
    return (y * g.astype(jnp.float32)).astype(x.dtype)

def layer_norm(x, g, b):
    xf = x.astype(jnp.float32)
    mu = jnp.mean(xf, axis=-1, keepdims=True)
    xc = xf - mu
    y = xc * lax.rsqrt(jnp.mean(xc * xc, axis=-1, keepdims=True) + LN_EPS)
    return (y * g.astype(jnp.float32) + b.astype(jnp.float32)).astype(x.dtype)

def t5_bucket(rel):
    half = N_REL_BUCKETS // 2
    max_exact = half // 2
    ret = jnp.where(rel > 0, half, 0)
    n = jnp.abs(rel)
    nf = jnp.maximum(n, 1).astype(jnp.float32)
    large = max_exact + (jnp.log(nf / max_exact) / math.log(REL_MAX_DISTANCE / max_exact)
                         * (half - max_exact)).astype(jnp.int32)
    large = jnp.minimum(large, half - 1)
    return ret + jnp.where(n < max_exact, n, large)

def dilated_window_branch(q, k, v, rel_bias, window, dil):
    B, S, H, Dh = q.shape
    half = window // (2 * dil)
    blk = half
    L = S // dil
    nb = -(-L // blk)
    Lp = nb * blk

    def to_blocks(t):
        t = t.reshape(B, L, dil, H, Dh).transpose(0, 2, 1, 3, 4)
        t = jnp.pad(t, ((0, 0), (0, 0), (0, Lp - L), (0, 0), (0, 0)))
        return t.reshape(B, dil, nb, blk, H, Dh)

    def neighbourhood(t):
        tp = jnp.pad(t, ((0, 0), (0, 0), (1, 1), (0, 0), (0, 0), (0, 0)))
        return jnp.concatenate([tp[:, :, :-2], tp[:, :, 1:-1], tp[:, :, 2:]], axis=3)

    qb = to_blocks(q)
    kw = neighbourhood(to_blocks(k))
    vw = neighbourhood(to_blocks(v))

    q_local = jnp.arange(blk)
    k_local = jnp.arange(3 * blk) - blk
    rel = k_local[None, :] - q_local[:, None]
    bias = rel_bias[t5_bucket(rel * dil)].astype(jnp.float32)
    k_idx = jnp.arange(nb)[:, None] * blk + k_local[None, :]
    valid = (jnp.abs(rel) <= half)[None] & ((k_idx >= 0) & (k_idx < L))[:, None, :]

    s = jnp.einsum('brnqhd,brnkhd->brnhqk', qb, kw).astype(jnp.float32)
    s = s + bias.transpose(2, 0, 1)
    s = jnp.where(valid[:, None], s, NEG_INF)
    m = jnp.max(s, axis=-1, keepdims=True)
    p = jnp.exp(s - m)
    den = jnp.sum(p, axis=-1, keepdims=True)
    o = jnp.einsum('brnhqk,brnkhd->brnqhd', (p / den).astype(v.dtype), vw)
    lse = (m + jnp.log(den))[..., 0].transpose(0, 1, 2, 4, 3)

    o = o.reshape(B, dil, Lp, H, Dh)[:, :, :L].transpose(0, 2, 1, 3, 4).reshape(B, S, H, Dh)
    lse = lse.reshape(B, dil, Lp, H)[:, :, :L].transpose(0, 2, 1, 3).reshape(B, S, H)
    return o, lse

def dilated_attention(q, k, v, rel_bias):
    outs, lses = [], []
    for window, dil in DILATED_BRANCHES:
        o, l = dilated_window_branch(q, k, v, rel_bias, window, dil)
        outs.append(o)
        lses.append(l)
    w = jax.nn.softmax(jnp.stack(lses, axis=0), axis=0)
    return jnp.einsum('ibsh,ibshd->bshd', w.astype(q.dtype), jnp.stack(outs, axis=0))

def spatial_gating(u, v, ln_g, ln_b, w_s, b_s):
    B, S, _ = u.shape
    nc = S // SGU_CHUNK
    v = layer_norm(v, ln_g, ln_b).reshape(B, nc, SGU_CHUNK, N_SGU_GROUPS, SGU_GROUP_DIM)
    mixed = jnp.einsum('gts,bnsgc->bntgc', w_s, v) + b_s.T[None, None, :, :, None]
    return u * mixed.reshape(B, S, D_SGU)

def hybrid_layer(x, g_pre_mix, w_in, sgu_ln_g, sgu_ln_b, sgu_w, sgu_b, w_out, g_post_mix,
                 g_pre_ffn, w_ff1, w_ff2, g_post_ffn, rel_bias):
    B, S, _ = x.shape
    h = rms_norm(x, g_pre_mix)
    z = h @ w_in
    q, k, v, zu, zv = jnp.split(
        z, [D_ATTN, 2 * D_ATTN, 3 * D_ATTN, 3 * D_ATTN + D_SGU], axis=-1)
    q = q.reshape(B, S, N_ATTN_HEADS, HEAD_DIM) * (HEAD_DIM ** -0.5)
    k = k.reshape(B, S, N_ATTN_HEADS, HEAD_DIM)
    v = v.reshape(B, S, N_ATTN_HEADS, HEAD_DIM)
    attn = dilated_attention(q, k, v, rel_bias).reshape(B, S, D_ATTN)
    sgu = spatial_gating(jax.nn.gelu(zu), jax.nn.gelu(zv), sgu_ln_g, sgu_ln_b, sgu_w, sgu_b)
    mix = jnp.concatenate([attn, sgu], axis=-1) @ w_out
    x = x + rms_norm(mix, g_post_mix)
    h = rms_norm(x, g_pre_ffn)
    f = jnp.square(jax.nn.relu(h @ w_ff1)) @ w_ff2
    return x + rms_norm(f, g_post_ffn)

def first_inputs(seed: int = 0) -> dict:
    key = jax.random.key(seed)
    ks = jax.random.split(key, 16)
    f32 = jnp.float32

    def nrm(k, shape, scale):
        return jax.random.normal(k, shape, f32) * scale

    def gain(k, shape):
        return 1.0 + 0.05 * jax.random.normal(k, shape, f32)

    return {
        "x": jax.random.normal(ks[0], (BATCH, SEQ, D_MODEL), f32),
        "g_pre_mix": gain(ks[1], (DEPTH, D_MODEL)),
        "w_in": nrm(ks[2], (DEPTH, D_MODEL, D_IN_PROJ), D_MODEL ** -0.5),
        "sgu_ln_g": gain(ks[3], (DEPTH, D_SGU)),
        "sgu_ln_b": nrm(ks[4], (DEPTH, D_SGU), 0.02),
        "sgu_w": nrm(ks[5], (DEPTH, N_SGU_GROUPS, SGU_CHUNK, SGU_CHUNK), SGU_CHUNK ** -0.5),
        "sgu_b": gain(ks[6], (DEPTH, N_SGU_GROUPS, SGU_CHUNK)),
        "w_out": nrm(ks[7], (DEPTH, D_MIX, D_MODEL), D_MIX ** -0.5),
        "g_post_mix": gain(ks[8], (DEPTH, D_MODEL)),
        "g_pre_ffn": gain(ks[9], (DEPTH, D_MODEL)),
        "w_ff1": nrm(ks[10], (DEPTH, D_MODEL, D_FF), D_MODEL ** -0.5),
        "w_ff2": nrm(ks[11], (DEPTH, D_FF, D_MODEL), D_FF ** -0.5),
        "g_post_ffn": gain(ks[12], (DEPTH, D_MODEL)),
        "rel_bias": nrm(ks[13], (N_REL_BUCKETS, N_ATTN_HEADS), 0.5),
    }

def first_block(x, g_pre_mix, w_in, sgu_ln_g, sgu_ln_b, sgu_w, sgu_b, w_out, g_post_mix,
              g_pre_ffn, w_ff1, w_ff2, g_post_ffn, rel_bias):
    for layer in range(DEPTH):
        x = hybrid_layer(x, g_pre_mix[layer], w_in[layer], sgu_ln_g[layer], sgu_ln_b[layer],
                         sgu_w[layer], sgu_b[layer], w_out[layer], g_post_mix[layer],
                         g_pre_ffn[layer], w_ff1[layer], w_ff2[layer], g_post_ffn[layer],
                         rel_bias)
    return x


N_HEADS = 8
N_KV_HEADS = 2
ATTN_WIDTH = N_HEADS * HEAD_DIM
CONV_CH = D_MODEL - ATTN_WIDTH
N_IDX_HEADS = 8
IDX_DIM = 64
TOPK_MAX = 256
CONV_K = 31
D_FF_2 = 4 * D_MODEL
ROPE_THETA = 500000.0
Q_BLOCK = 128
EPS = 1e-6
SPLITS = (ATTN_WIDTH, N_KV_HEADS * HEAD_DIM, N_KV_HEADS * HEAD_DIM,
          N_IDX_HEADS * IDX_DIM, IDX_DIM, N_IDX_HEADS, 2 * CONV_CH)
D_IN = ATTN_WIDTH + 4 * N_KV_HEADS * HEAD_DIM // 2 + N_IDX_HEADS * IDX_DIM + IDX_DIM + N_IDX_HEADS + 2 * CONV_CH


def _rmsnorm(x, g):
    xf = x.astype(jnp.float32)
    y = xf * lax.rsqrt(jnp.mean(xf * xf, axis=-1, keepdims=True) + EPS)
    return (y * g.astype(jnp.float32)).astype(x.dtype)

def _layernorm(x, g, b):
    xf = x.astype(jnp.float32)
    mu = jnp.mean(xf, axis=-1, keepdims=True)
    var = jnp.mean(jnp.square(xf - mu), axis=-1, keepdims=True)
    y = (xf - mu) * lax.rsqrt(var + EPS)
    return (y * g.astype(jnp.float32) + b.astype(jnp.float32)).astype(x.dtype)

def _partial_rope(x, positions):
    d = x.shape[-1]
    rot = d // 4
    half = rot // 2
    inv_freq = jnp.power(ROPE_THETA, -jnp.arange(half, dtype=jnp.float32) * 2.0 / rot)
    ang = positions.astype(jnp.float32)[:, :, None] * inv_freq
    cos = jnp.cos(ang)[:, :, None, :]
    sin = jnp.sin(ang)[:, :, None, :]
    xf = x.astype(jnp.float32)
    x1, x2, rest = xf[..., :half], xf[..., half:rot], xf[..., rot:]
    out = jnp.concatenate([x1 * cos - x2 * sin, x2 * cos + x1 * sin, rest], axis=-1)
    return out.astype(x.dtype)

def _dsa_attention(q, k, v, q_idx, k_idx, w_idx):
    B, S = q.shape[0], q.shape[1]
    nb = S // Q_BLOCK
    topk = min(TOPK_MAX, S // 4)
    groups = N_HEADS // N_KV_HEADS
    key_pos = jnp.arange(S, dtype=jnp.int32)

    def to_blocks(a):
        a = a.reshape((B, nb, Q_BLOCK) + a.shape[2:])
        return jnp.moveaxis(a, 1, 0)

    xs = (to_blocks(q), to_blocks(q_idx), to_blocks(w_idx),
          key_pos.reshape(nb, Q_BLOCK))

    def block_fn(blk):
        qb, qib, wb, tb = blk
        logits = jnp.einsum('bthd,bsd->bths', qib.astype(jnp.float32),
                            k_idx.astype(jnp.float32)) * (IDX_DIM ** -0.5)
        score = jnp.einsum('bth,bths->bts', wb.astype(jnp.float32), jax.nn.relu(logits))
        causal = key_pos[None, :] <= tb[:, None]
        score = jnp.where(causal[None], score, -jnp.inf)
        _, sel = lax.top_k(score, topk)
        sel_ok = sel <= tb[None, :, None]
        k_sel = jax.vmap(lambda kb, ib: kb[ib])(k, sel)
        v_sel = jax.vmap(lambda vb, ib: vb[ib])(v, sel)
        qg = qb.reshape(B, Q_BLOCK, N_KV_HEADS, groups, HEAD_DIM)
        s = jnp.einsum('btkgd,btnkd->btkgn', qg, k_sel).astype(jnp.float32) * (HEAD_DIM ** -0.5)
        s = jnp.where(sel_ok[:, :, None, None, :], s, -jnp.inf)
        p = jax.nn.softmax(s, axis=-1).astype(v.dtype)
        o = jnp.einsum('btkgn,btnkd->btkgd', p, v_sel)
        return o.reshape(B, Q_BLOCK, ATTN_WIDTH)

    out = lax.map(block_fn, xs)
    return jnp.moveaxis(out, 0, 1).reshape(B, S, ATTN_WIDTH)

def _conformer_conv(u, conv_w, conv_b, norm_g, norm_b):
    a, g = jnp.split(u, 2, axis=-1)
    glu = a * jax.nn.sigmoid(g)
    y = lax.conv_general_dilated(
        glu, conv_w[:, None, :], window_strides=(1,),
        padding=[(CONV_K - 1, 0)],
        dimension_numbers=('NWC', 'WIO', 'NWC'),
        feature_group_count=CONV_CH) + conv_b
    y = _layernorm(y, norm_g, norm_b)
    return jax.nn.silu(y)

def second_inputs(seed: int = 0) -> dict:
    key = jax.random.key(seed)
    ks = jax.random.split(key, 20)
    f32 = jnp.float32
    nrm = lambda k, shp, s: jax.random.normal(k, shp, f32) * s
    x = jax.random.normal(ks[0], (BATCH, SEQ, D_MODEL), f32)
    c = jax.random.normal(ks[1], (BATCH, D_MODEL), f32)
    offset = jax.random.randint(ks[2], (BATCH, 1), 0, 1024, dtype=jnp.int32)
    positions = offset + jnp.arange(SEQ, dtype=jnp.int32)[None, :]
    return {
        "x": x,
        "c": c,
        "positions": positions,
        "w_ada": nrm(ks[3], (DEPTH, D_MODEL, 6 * D_MODEL), 0.5 * D_MODEL ** -0.5),
        "b_ada": nrm(ks[4], (DEPTH, 6 * D_MODEL), 0.01),
        "g_mix": 1.0 + nrm(ks[5], (DEPTH, D_MODEL), 0.02),
        "w_in": nrm(ks[6], (DEPTH, D_MODEL, D_IN), D_MODEL ** -0.5),
        "conv_w": nrm(ks[7], (DEPTH, CONV_K, CONV_CH), CONV_K ** -0.5),
        "conv_b": nrm(ks[8], (DEPTH, CONV_CH), 0.01),
        "conv_norm_g": 1.0 + nrm(ks[9], (DEPTH, CONV_CH), 0.02),
        "conv_norm_b": nrm(ks[10], (DEPTH, CONV_CH), 0.01),
        "w_out": nrm(ks[11], (DEPTH, D_MODEL, D_MODEL), D_MODEL ** -0.5),
        "g_mlp": 1.0 + nrm(ks[12], (DEPTH, D_MODEL), 0.02),
        "w_up": nrm(ks[13], (DEPTH, D_MODEL, D_FF_2), D_MODEL ** -0.5),
        "w_down": nrm(ks[14], (DEPTH, D_FF_2, D_MODEL), D_FF_2 ** -0.5),
        "g_final": 1.0 + nrm(ks[15], (D_MODEL,), 0.02),
    }

def second_block(x, c, positions, w_ada, b_ada, g_mix, w_in, conv_w, conv_b,
              conv_norm_g, conv_norm_b, w_out, g_mlp, w_up, w_down, g_final):
    B, S, _ = x.shape
    split_at = [int(i) for i in np.cumsum(SPLITS)[:-1]]
    cond = jax.nn.silu(c)
    for i in range(DEPTH):
        mod = jnp.einsum('bd,de->be', cond, w_ada[i]) + b_ada[i]
        sh1, sc1, gt1, sh2, sc2, gt2 = jnp.split(mod, 6, axis=-1)

        h = _rmsnorm(x, g_mix[i]) * (1.0 + sc1[:, None, :]) + sh1[:, None, :]
        proj = jnp.einsum('bsd,de->bse', h, w_in[i])
        q, k, v, qi, ki, wi, cu = jnp.split(proj, split_at, axis=-1)
        q = _partial_rope(q.reshape(B, S, N_HEADS, HEAD_DIM), positions)
        k = _partial_rope(k.reshape(B, S, N_KV_HEADS, HEAD_DIM), positions)
        v = v.reshape(B, S, N_KV_HEADS, HEAD_DIM)
        qi = _partial_rope(qi.reshape(B, S, N_IDX_HEADS, IDX_DIM), positions)
        ki = _partial_rope(ki.reshape(B, S, 1, IDX_DIM), positions)[:, :, 0, :]
        wi = wi * (N_IDX_HEADS ** -0.5)
        attn_out = _dsa_attention(q, k, v, qi, ki, wi)
        conv_out = _conformer_conv(cu, conv_w[i], conv_b[i],
                                   conv_norm_g[i], conv_norm_b[i])
        mixed = jnp.concatenate([attn_out, conv_out], axis=-1)
        x = x + gt1[:, None, :] * jnp.einsum('bse,ed->bsd', mixed, w_out[i])

        h = _rmsnorm(x, g_mlp[i]) * (1.0 + sc2[:, None, :]) + sh2[:, None, :]
        u = jnp.square(jax.nn.relu(jnp.einsum('bsd,df->bsf', h, w_up[i])))
        x = x + gt2[:, None, :] * jnp.einsum('bsf,fd->bsd', u, w_down[i])
    return _rmsnorm(x, g_final)


def setup_inputs(seed=0):
    out = dict(first_inputs(seed))
    for name, value in second_inputs(seed + 1).items():
        if name != "x":
            out[name + "_2"] = value
    return out


def reference(
    x, g_pre_mix, w_in, sgu_ln_g, sgu_ln_b, sgu_w, sgu_b, w_out, g_post_mix, g_pre_ffn, w_ff1,
    w_ff2, g_post_ffn, rel_bias, c_2, positions_2, w_ada_2, b_ada_2, g_mix_2, w_in_2, conv_w_2,
    conv_b_2, conv_norm_g_2, conv_norm_b_2, w_out_2, g_mlp_2, w_up_2, w_down_2, g_final_2,
):
    x = first_block(
        x, g_pre_mix, w_in, sgu_ln_g, sgu_ln_b, sgu_w, sgu_b, w_out, g_post_mix, g_pre_ffn,
        w_ff1, w_ff2, g_post_ffn, rel_bias,
    )
    return second_block(
        x, c_2, positions_2, w_ada_2, b_ada_2, g_mix_2, w_in_2, conv_w_2, conv_b_2,
        conv_norm_g_2, conv_norm_b_2, w_out_2, g_mlp_2, w_up_2, w_down_2, g_final_2,
    )


_drawn_inputs = setup_inputs


def setup_inputs(seed=0):
    import zlib

    import numpy as np

    out = dict(_drawn_inputs(seed))
    spreads = {}
    factors = {'sgu_ln_b': 5.699,
     'b_ada_2': 6.038,
     'g_mix_2': 8.0,
     'conv_b_2': 56.694,
     'conv_norm_g_2': 44.689,
     'conv_norm_b_2': 64.0,
     'g_mlp_2': 8.0,
     'g_final_2': 8.408}
    for name, (base, spread) in spreads.items():
        noise = np.random.default_rng([zlib.crc32(name.encode()), seed]).standard_normal(out[name].shape)
        drawn = base * np.exp(spread * noise) if base else spread * noise
        out[name] = __import__('jax').numpy.asarray(drawn.astype(out[name].dtype))
    for name, factor in factors.items():
        out[name] = (out[name] * factor).astype(out[name].dtype)
    return out
```

```python
from contextlib import ExitStack

import numpy as np

import concourse.bass as bass
from concourse import mybir

F32 = mybir.dt.float32
F32R = mybir.dt.float32r
BF16 = mybir.dt.bfloat16
U32 = mybir.dt.uint32
U8 = mybir.dt.uint8
I32 = mybir.dt.int32
ACT = mybir.ActivationFunctionType
ALU = mybir.AluOpType
AX = mybir.AxisListType

P = 128
S = 1024
D = 1024
KT_N = D // P
HALF = 512
NT = S // P
DH = 64
HEADS = 8
ATT = HEADS * DH
D_FF = 4 * D
GROUPS = D_FF // D
TOPK = 256
TOPK_TILE = TOPK // P
CONV_K = 31
PAD = CONV_K - 1
SGU_G = 8
FAR = -1e30
HIGHEST = 3.4028234e38
LOWEST = -HIGHEST
RMS_EPS = 1e-6
SGU_EPS = 1e-5
BITS = 31

IN1, N_IN1 = 0, 20
OUT1 = IN1 + N_IN1
FFN1 = OUT1 + 8
IN2, N_IN2 = FFN1 + 16 * GROUPS, 19
OUT2 = IN2 + N_IN2
FFN2 = OUT2 + 8
SLABS = FFN2 + 16 * GROUPS
STREAM = SLABS + 1
S_KI, S_QI, S_Q, S_K, S_V, S_CONV = 0, 1, 5, 9, 10, 11

VECS = [("g_pre_mix", 8), ("g_post_mix", 8), ("g_pre_ffn", 8), ("g_post_ffn", 8), ("sgu_b", 8), ("b_ada", 48),
        ("g_mix", 8), ("conv_w", 4 * CONV_K), ("conv_b", 4), ("conv_g", 4), ("conv_nb", 4), ("g_mlp", 8),
        ("g_final", 8), ("c", 8)]
VCOL, _n = {}, 0
for _name, _k in VECS:
    VCOL[_name] = _n
    _n += _k
N_VEC = _n

A_VEC = 16544
A_CONST = A_VEC + 4 * N_VEC
N_CONST = 4 * P + 1
A_SMALL = A_CONST + 4 * N_CONST + 28
A_RAW = A_SMALL + 2560
A_WHI = A_RAW + 8192
A_WLO = A_WHI + 8192
A_XT = A_WLO + 8192
A_XH = A_XT + 32768
A_XL = A_XH + 32768
A_R = A_XL + 32768
N_SCORE = sum(P * (i + 1) for i in range(TOPK_TILE, NT))


def score_at(i):
    return sum(P * (j + 1) for j in range(TOPK_TILE, i))


def t5_tables():
    n_rel = 2 * S
    hot = np.zeros((33, n_rel), np.float32)
    for col in range(n_rel):
        rel = col - S
        n = abs(rel)
        if n < 8:
            bucket = n
        else:
            bucket = min(8 + int(np.floor(np.log(n / 8) / np.log(1024 / 8) * 8)), 15)
        if rel > 0:
            bucket += 16
        hot[bucket, col] = 1.0
        seen = (n <= 64) + (n % 4 == 0 and n <= 256) + (n % 16 == 0 and n <= 1024)
        hot[32, col] = np.log(seen) if seen else FAR
    return hot


class Tally:

    def __init__(self, sem, n=0):
        self.sem, self.n = sem, n

    def inc(self, ins):
        self.n += 1
        ins.then_inc(self.sem, 1)

    def wait(self, eng, by=0):
        self.n += by
        if self.n > 0:
            eng.wait_ge(self.sem, self.n)


def build(nc, slabs, ada, xT, vecs, lnrow, sgu_wT, rel_bias, positions, consts, hot, outT, dbg=None):
    ctx = ExitStack()

    def at(name, shape, off, dt=F32):
        return nc.alloc_sbuf_tensor_at(name, shape, dt, offset=off)

    def sem(name):
        return ctx.enter_context(nc.semaphore(name))

    vec = at("vec", [P, N_VEC], A_VEC)
    cst = at("cst", [P, N_CONST], A_CONST)
    ident, swap, ones, flip = (cst[:, n * P:(n + 1) * P] for n in range(4))
    freq = cst[:, 4 * P:4 * P + 1]

    small_at = [A_SMALL]

    def small(name, n, dt=F32):
        t = at(name, [P, n], small_at[0], dt)
        small_at[0] += -(-4 * n // 32) * 32
        assert small_at[0] <= A_RAW
        return t

    raw = [at(f"raw{b}", [P, S], A_RAW + 4096 * b) for b in range(2)]
    whi = [at(f"whi{b}", [P, KT_N, P], A_WHI + 4096 * b, F32R) for b in range(2)]
    wlo = [at(f"wlo{b}", [P, KT_N, P], A_WLO + 4096 * b, F32R) for b in range(2)]
    XT = at("XT", [P, KT_N, S], A_XT)
    XH = at("XH", [P, KT_N, S], A_XH, F32R)
    XL = at("XL", [P, KT_N, S], A_XL, F32R)

    NORM0 = A_R + 32768
    SQ = [at(f"SQ{b}", [P, S], NORM0 + 4096 * b) for b in range(2)]
    SSQ = at("SSQ", [P, S], NORM0 + 8192)
    DG = at("DG", [P, NT, P], NORM0 + 12288)
    HF = [at(f"HF{b}", [P, S], NORM0 + 16384 + 4096 * b) for b in range(2)]
    XRE = at("XRE", [P, 4, S], NORM0 + 24576)
    ACC = at("ACC", [P, KT_N, S], A_R)

    QT = at("QT", [P, 4, S], A_R)
    KT = at("KT", [P, 4, S], A_R + 16384)
    NAT = at("NAT", [P, 3, NT, ATT], A_R + 32768)
    TT = [at(f"TT{b}", [P, S], A_XT + 4096 * b) for b in range(2)]
    BIAS = [at(f"BIAS{b}", [P, 1920], A_XT + 8192 + 7680 * b) for b in range(2)]
    TAB = at("TAB", [P, 2 * S], A_XL + 0)
    HOT = at("HOT", [P, 2 * S], A_XL + 8192)
    LNG = at("LNG", [P, 2, ATT], A_XL)
    SGW = at("SGW", [P, SGU_G, P], A_XL + 4096)
    PB = [at(f"PB{b}", [P, S], A_XH + 4096 * b) for b in range(3)]
    PTS = [at(f"PTS{b}", [P, S], A_XH + 24576 + 4096 * b) for b in range(2)]
    NATA = at("NATA", [P, NT, ATT], A_XL + 16384)
    UH = at("UH", [P, KT_N, S], A_R, F32R)
    UL = at("UL", [P, KT_N, S], A_R + 32768, F32R)
    RELU = at("RELU", [P, S], A_R + 65536)
    USQ = at("USQ", [P, S], A_R + 65536 + 4096)
    ADA = [at(f"ADA{b}", [P, KT_N, P], A_R + 65536 + 8192 + 4096 * b) for b in range(2)]
    RED = [at(f"RED{b}", [P, P], A_R + 65536 + 16384 + 512 * b) for b in range(2)]
    o = A_R
    QT2 = at("QT2", [P, 4, S], o); o += 16384
    KT2 = at("KT2", [P, S], o); o += 4096
    V2 = at("V2", [P, NT, P], o); o += 4096
    QI = at("QI", [P, 4, S], o); YC = at("YC", [P, 4, S], o); o += 16384
    KI = at("KI", [P, S], o); o += 4096
    SC = at("SC", [P, N_SCORE], o); o += 4 * N_SCORE
    MASK01 = at("MASK01", [P, 3 * P], o); o += 4 * 3 * P
    COS = at("COS", [P, S], o); o += 4096
    SIN = at("SIN", [P, S], o); o += 4096
    T2 = [at(f"T2_{b}", [P, S], o + 4096 * b) for b in range(2)]; o += 8192
    T1 = at("T1", [P, S], o); o += 4096
    assert o <= nc.sbuf_usable_end
    SQ2 = [at(f"SQ2_{b}", [P, S], A_R + 4096 * b) for b in range(2)]
    SSQ2 = at("SSQ2", [P, S], A_R + 8192)
    DG2 = at("DG2", [P, NT, P], A_R + 12288)
    HC = [at(f"HC{b}", [P, S], A_R + 45056 + 4096 * b) for b in range(2)]
    o = A_XT
    CU = at("CU", [P, 4, S + PAD], o); o += 16 * (S + PAD)
    SIG = at("SIG", [P, S], o); o += 4096
    JUNK = at("JUNK", [P, 2, S], o, U8); o += 2 * S
    TK1 = at("TK1", [P, S], o); POSI = at("POSI", [P, S], o, I32); o += 4096
    TK2 = at("TK2", [P, S], o); o += 4096
    assert o <= A_XH

    G = [nc.alloc_psum_tensor(f"G{b}", [P, 2, HALF], F32) for b in range(2)]
    TP = [nc.alloc_psum_tensor(f"TP{b}", [P, 2, HALF], F32) for b in range(2)]

    x_spill = nc.dram_tensor("x_spill", [D, S], F32, kind="Internal").ap()
    tab_spill = nc.dram_tensor("tab_spill", [HEADS * 2 * S], F32, kind="Internal").ap()
    tiled = lambda t: t.rearrange("(k p) t -> p k t", p=P)
    xT_v, spill_v, out_v = tiled(xT), tiled(x_spill), tiled(outT)

    RB = small("RB", 8)
    var = small("var", NT)
    root = small("root", NT)
    y0 = small("y0", NT)
    aa = small("aa", NT)
    rstd = small("rstd", NT)
    negm = small("negm", 3)
    den = small("den", 4)
    rden = small("rden", 2)
    bn6 = small("bn6", NT * 6)
    mv = small("mv", NT * 2)
    mod = small("mod", 48)
    scl = small("scl", 16)
    silc = small("silc", 8)
    wi = small("wi", NT * 8)
    NQ = NT - TOPK_TILE
    sgn = small("sgn", NQ)
    need = small("need", NQ)
    cnt = small("cnt", NQ)
    keep = small("keep", NQ, U32)
    mag = small("mag", NQ, U32)
    cand = small("cand", NQ, U32)
    thr = small("thr", NQ)

    raw_loaded = [sem(f"raw_loaded{b}") for b in range(2)]
    hi_ready, lo_ready = sem("hi_ready"), sem("lo_ready")
    slab_done = sem("slab_done")
    psum_free = [sem(f"psum_free{b}") for b in range(2)]
    params_loaded, x_loaded, sgu_loaded = sem("params_loaded"), sem("x_loaded"), sem("sgu_loaded")
    hot_loaded, tab_made, tab_stored = sem("hot_loaded"), sem("tab_made"), sem("tab_stored")
    tab_copied = sem("tab_copied")
    bias_loaded = [sem(f"bias_loaded{b}") for b in range(2)]
    x_hi, x_split = sem("x_hi"), sem("x_split")
    turned_in, turned, turn_out = sem("turned_in"), sem("turned"), sem("turn_out")
    sq_ready, sq_used = sem("sq_ready"), sem("sq_used")
    stat_ready, var_ready, root_ready = sem("stat_ready"), sem("var_ready"), sem("root_ready")
    diag_ready, spread_ready, hf_ready = sem("diag_ready"), sem("spread_ready"), sem("hf_ready")
    scores_ready, masked, exped = sem("scores_ready"), sem("masked"), sem("exped")
    half_turned, pt_a, pt_b = sem("half_turned"), sem("pt_a"), sem("pt_b")
    pv_done, att_out = sem("pv_done"), sem("att_out")
    mixed_ready, mixed_mm, gated = sem("mixed_ready"), sem("mixed_mm"), sem("gated")
    dve_seq, act_seq, pool_seq = sem("dve_seq"), sem("act_seq"), sem("pool_seq")
    xre_loaded = [sem(f"xre_loaded{b}") for b in range(4)]
    xt_ready = sem("xt_ready")
    spilled, x_back = sem("spilled"), sem("x_back")
    usq_ready, u_hi, u_split = sem("usq_ready"), sem("u_hi"), sem("u_split")
    ada_loaded = [sem(f"ada_loaded{b}") for b in range(2)]
    ada_prod, ada_red, mod_col, mod_ready = sem("ada_prod"), sem("ada_red"), sem("mod_col"), sem("mod_ready")
    silc_ready = sem("silc_ready")
    pos_loaded, angle_ready, rope_ready = sem("pos_loaded"), sem("angle_ready"), sem("rope_ready")
    swapped, roped = sem("swapped"), sem("roped")
    raw_copied = sem("raw_copied")
    ki_doubled, wi_turned, wi_ready = sem("ki_doubled"), sem("wi_turned"), sem("wi_ready")
    idx_scores, idx_relu, idx_added, idx_masked = sem("idx_scores"), sem("idx_relu"), sem("idx_added"), sem("idx_masked")
    v2_turned, v2_ready = sem("v2_turned"), sem("v2_ready")
    cu_raw, sig_ready, glu_ready = sem("cu_raw"), sem("sig_ready"), sem("glu_ready")
    conv_ready, conv_mean, conv_centred = sem("conv_ready"), sem("conv_mean"), sem("conv_centred")
    cleared, out_stored, mask01 = sem("cleared"), sem("out_stored"), sem("mask01")

    def V(name, k=0):
        c = VCOL[name] + k
        return vec[:, c:c + 1]

    flat = lambda t: t[:, :, :].rearrange("p a b -> p (a b)")
    Gf, TPf = [flat(t) for t in G], [flat(t) for t in TP]

    UNITS1 = [(i, h, NT) for h in range(HEADS) for i in range(NT)]
    UNITS2 = [(i, h, i + 1) for i in range(NT) for h in range(HEADS)]
    UNITS = UNITS1 + UNITS2
    n_b = [0]
    n_half = [0]
    for _, _, w in UNITS:
        n_b.append(n_b[-1] + (w > 4))
        n_half.append(n_half[-1] + 1 + (w > 4))

    def taken(g):
        return psum_free[g % 2], g // 2 + 2

    def slabs_of(eng, g0, first, last, body):
        pairs = (last - first) // 2
        if pairs >= 2:
            with eng.Fori(0, pairs) as t:
                for j in range(2):
                    g = g0 + first + j
                    body(t * 2 + (first + j), t * 2 + g, g % 2, t + g // 2)
            first += 2 * pairs
        for m in range(first, last):
            g = g0 + m
            body(m, g, g % 2, g // 2)

    N_HF_BEFORE_OUT = 8 * 4 + 4

    block = ctx.enter_context(nc.Block())

    @block.sync
    def _(sp):
        def load(g, b):
            sp.dma_start(raw[b][:, :], slabs[bass.ds(g, 1), :, :].rearrange("a p n -> p (a n)")
                         if not isinstance(g, int) else slabs[g, :, :]).then_inc(raw_loaded[b], 16)

        load(0, 0)
        sp.dma_start(vec[:, :], vecs).then_inc(params_loaded, 16)
        sp.dma_start(cst[:, :], consts).then_inc(params_loaded, 16)
        for k in range(KT_N):
            sp.dma_start(XT[:, k, :], xT_v[:, k, :]).then_inc(x_loaded, 16)
        load(1, 1)
        with sp.Fori(0, (STREAM - 2) // 2) as t:
            for j in range(2):
                sp.wait_ge(lo_ready, t * 2 + (1 + j))
                load(t * 2 + (2 + j), j)
        sp.wait_ge(out_stored, 16 * KT_N)

    @block.gpsimd
    def _(pool):
        pseq = Tally(pool_seq)
        pool.dma_start(HOT[0:33, :], hot).then_inc(hot_loaded, 16)
        pool.wait_ge(cleared, 1)
        pool.dma_start(RB[0:32, :], rel_bias).then_inc(hot_loaded, 16)
        pool.wait_ge(tab_copied, 1)
        pool.dma_start(tab_spill.rearrange("(h n) -> h n", h=HEADS), TAB[0:HEADS, :]).then_inc(tab_stored, 16)
        pool.wait_ge(tab_stored, 16)
        pool.wait_ge(slab_done, 1 + OUT1)

        def load_bias(h):
            src = bass.AP(tensor=tab_spill.tensor, offset=h * 2 * S + S - 896 - (P - 1),
                          ap=[[1, P], [1, 1920]])
            pool.dma_start(BIAS[h % 2][:, :], src).then_inc(bias_loaded[h % 2], 16)

        pool.dma_start(SGW[:, :, :], sgu_wT.rearrange("p (g t) -> p g t", g=SGU_G)).then_inc(sgu_loaded, 16)
        for r in range(2):
            pool.dma_start(LNG[:, r, :], lnrow[r:r + 1, :].broadcast_to([P, ATT])).then_inc(sgu_loaded, 16)
        for h in range(HEADS):
            if h >= 2:
                pool.wait_ge(masked, NT * (h - 1))
            load_bias(h)

        def residual_tiles(src):
            for k in range(KT_N):
                if k >= 4:
                    pool.wait_ge(xt_ready, base_xt[0] + k - 3)
                pool.dma_start(XRE[:, k % 4, :], src[:, k, :]).then_inc(xre_loaded[k % 4], 16)
            base_xt[0] += KT_N

        base_xt = [0]
        pool.wait_ge(x_split, 16)
        residual_tiles(xT_v)
        pool.wait_ge(xt_ready, KT_N)
        pool.dma_start(spill_v, XT[:, :, :]).then_inc(spilled, 16)

        def ada_load(a, b):
            pool.dma_start(ADA[b][:, :, :].rearrange("p k n -> p (k n)"),
                           ada[bass.ds(a, 1), :, :].rearrange("a p n -> p (a n)")
                           if not isinstance(a, int) else ada[a, :, :]).then_inc(ada_loaded[b], 16)

        pool.wait_ge(x_split, 24)
        pool.wait_ge(silc_ready, 1)
        ada_load(0, 0)
        ada_load(1, 1)
        with pool.Fori(0, 23) as t:
            for b in range(2):
                pool.wait_ge(ada_loaded[b], t * 16 + 16)
                pool.tensor_tensor(ADA[b][:, :, :], ADA[b][:, :, :],
                                   silc[:, :].unsqueeze(2).broadcast_to([P, KT_N, P]), ALU.mult).then_inc(ada_prod, 1)
                pool.wait_ge(ada_red, t * 2 + (1 + b))
                ada_load(t * 2 + (2 + b), b)
        for b in range(2):
            pool.wait_ge(ada_loaded[b], 16 * 24)
            pool.tensor_tensor(ADA[b][:, :, :], ADA[b][:, :, :],
                               silc[:, :].unsqueeze(2).broadcast_to([P, KT_N, P]), ALU.mult).then_inc(ada_prod, 1)
        pool.wait_ge(spilled, 16)
        pool.wait_ge(slab_done, 1 + IN2)
        residual_tiles(spill_v)
        pool.wait_ge(xt_ready, 2 * KT_N)
        pool.dma_start(spill_v, XT[:, :, :]).then_inc(spilled, 16)
        pool.wait_ge(x_split, 32)
        pool.wait_ge(spilled, 32)
        pool.dma_start(POSI[:, :], positions.broadcast_to([P, S])).then_inc(pos_loaded, 16)
        pool.memset(CU[:, :, 0:PAD], 0.0).then_inc(pool_seq, 1); pseq.n += 1
        pool.memset(MASK01[:, :], 0.0).then_inc(pool_seq, 1); pseq.n += 1
        pseq.wait(pool)
        for c in (0, 2):
            pool.affine_select(out=MASK01[:, c * P:(c + 1) * P], in_=MASK01[:, c * P:(c + 1) * P], compare_op=ALU.is_ge,
                               fill=-FAR, base=0, pattern=[[-1, P]], channel_multiplier=1).then_inc(mask01, 1)
        pool.wait_ge(roped, 1)
        pool.dma_start(KI[DH:P, :], KI[0:DH, :]).then_inc(ki_doubled, 16)
        for n, i in enumerate(range(TOPK_TILE, NT)):
            pool.wait_ge(idx_added, HEADS * (n + 1))
            c = score_at(i) + P * i
            pool.affine_select(out=SC[:, c:c + P], in_=SC[:, c:c + P], compare_op=ALU.is_ge,
                               fill=LOWEST, base=0, pattern=[[-1, P]], channel_multiplier=1).then_inc(idx_masked, 1)
        pool.wait_ge(conv_ready, 4)
        pool.dma_start(XT[:, :, :], spill_v).then_inc(x_back, 16)
        for k in range(KT_N):
            pool.wait_ge(hf_ready, N_HF_BEFORE_OUT + k + 1)
            pool.dma_start(out_v[:, k, :], XT[:, k, :]).then_inc(out_stored, 16)
        pool.wait_ge(out_stored, 16 * KT_N)

    @block.scalar
    def _(act):
        aseq = Tally(act_seq)
        t_sqi, t_squ = Tally(sq_ready), Tally(sq_used)
        t_var, t_root = Tally(var_ready), Tally(root_ready)
        t_hf = Tally(hf_ready)

        def hi(g, b, h):
            act.wait_ge(raw_loaded[b], h * 16 + 16)
            if not (isinstance(g, int) and g < 2):
                act.wait_ge(slab_done, g)
            act.activation(whi[b][:, :, :].rearrange("p k n -> p (k n)"), raw[b][:, :], ACT.Copy).then_inc(hi_ready, 1)

        def hi_next(g, b, h):
            hi(g + 1, 1 - b, h + (1 if b else 0))

        def squares(src, waits):
            for k in range(KT_N):
                act.wait_ge(*waits(k))
                if t_sqi.n >= 2:
                    act.wait_ge(sq_used, t_sqi.n - 1)
                t_sqi.inc(act.activation(SQ[k % 2][:, :], src(k), ACT.Square))

        def norm_root():
            t_var.wait(act, 1)
            t_root.inc(act.activation(root[:, :], var[:, :], ACT.Sqrt))

        def splits(n, dst, bias=None, func=ACT.Identity, scale=None):
            for k in range(n):
                t_hf.wait(act, 1)
                act.activation(XH[:, dst + k, :], HF[k % 2][:, :], ACT.Identity,
                               bias=bias(k) if bias else 0.0).then_inc(x_hi, 1)

        act.wait_ge(params_loaded, 32)
        hi(0, 0, 0)
        squares(lambda k: XT[:, k, :], lambda k: (x_loaded, 16 * KT_N))
        norm_root()
        act.wait_ge(params_loaded, 32)
        act.activation(silc[:, :], vec[:, VCOL["c"]:VCOL["c"] + 8], ACT.Silu).then_inc(silc_ready, 1)
        splits(KT_N, 0)

        def to_qk(dst, scale, off):
            def body(m, g, b, h):
                hi_next(g, b, h)
                act.wait_ge(slab_done, g + 2)
                act.activation(dst[:, bass.ds(m + (-off), 1), :].rearrange("p a t -> p (a t)")
                               if not isinstance(m, int) else dst[:, m - off, :],
                               Gf[b], ACT.Copy, scale=scale).then_inc(psum_free[b], 1)
            return body

        for m in range(4):
            hi_next(IN1 + m, m % 2, m // 2)
            act.wait_ge(slab_done, IN1 + m + 2)
            act.activation(QT[:, m, :].rearrange("p (t c) -> p t c", c=P)[:, :, ::-1],
                           Gf[m % 2].rearrange("p (t c) -> p t c", c=P), ACT.Copy,
                           scale=-DH ** -0.5).then_inc(psum_free[m % 2], 1)
        slabs_of(act, IN1, 4, 8, to_qk(KT, 1.0, 4))

        def to_tt(func):
            def body(m, g, b, h):
                hi_next(g, b, h)
                act.wait_ge(slab_done, g + 2)
                if not (isinstance(m, int) and m < 10):
                    act.wait_ge(turned, m + (-9))
                act.activation(TT[b][:, :], Gf[b], func).then_inc(psum_free[b], 1)
            return body

        slabs_of(act, IN1, 8, 10, to_tt(ACT.Copy))
        slabs_of(act, IN1, 10, 12, to_tt(ACT.Copy))
        slabs_of(act, IN1, 12, 20, to_tt(ACT.Gelu_apprx_tanh))

        norm_root()

        def attention(n0, n1):
            def exp(n):
                w = UNITS[n][2] * P
                act.wait_ge(masked, n + 1)
                act.activation(PB[n % 3][:, 0:w], PB[n % 3][:, 0:w], ACT.Exp, bias=negm[:, n % 3:n % 3 + 1], scale=-1.0,
                               accum_out=den[:, n % 4:n % 4 + 1]).then_inc(exped, 1)

            def copy_a(n):
                w = min(UNITS[n][2], 4) * P
                act.wait_ge(half_turned, n_half[n] + 1)
                if n >= 2:
                    act.wait_ge(pv_done, n - 1)
                act.activation(PTS[n % 2][:, 0:w], TPf[0][:, 0:w], ACT.Copy).then_inc(pt_a, 1)

            for n in range(n0, n1 + 2):
                if n < n1:
                    exp(n)
                if n >= n0 + 2:
                    copy_a(n - 2)

        attention(0, 64)

        def turned_hi(k0, n, base):
            for k in range(n):
                act.wait_ge(turned, base + k + 1)
                act.activation(XH[:, k0 + k, :], TPf[(base + k) % 2], ACT.Copy).then_inc(x_hi, 1)

        turned_hi(0, 8, 12)

        def only_hi(m, g, b, h):
            hi_next(g, b, h)

        slabs_of(act, OUT1, 0, 8, only_hi)
        squares(lambda k: ACC[:, k, :], lambda k: taken(OUT1 + k))
        norm_root()
        squares(lambda k: XT[:, k, :], lambda k: (xt_ready, 1 + k))
        norm_root()
        splits(KT_N, 0)

        def ffn(g0, which):
            with act.Fori(0, GROUPS) as grp:
                for m in range(16):
                    g, b = g0 + m, (g0 + m) % 2
                    h = grp * 8 + g // 2
                    hi(grp * 16 + (g + 1), 1 - b, h + (1 if b else 0))
                    if m < 8:
                        u = grp * 8 + (32 * which + m)
                        act.wait_ge(slab_done, grp * 16 + (g + 2))
                        act.wait_ge(usq_ready, u + 1)
                        act.activation(RELU[:, :], Gf[b], ACT.Relu).then_inc(psum_free[b], 1)
                        act.wait_ge(usq_ready, u + 2)
                        act.activation(UH[:, m, :], USQ[:, :], ACT.Copy).then_inc(u_hi, 1)

        ffn(FFN1, 0)
        act.wait_ge(slab_done, 1 + IN2)
        squares(lambda k: XT[:, k, :], lambda k: taken(IN2 - KT_N + k))
        norm_root()
        squares(lambda k: XT[:, k, :], lambda k: (xt_ready, 1 + KT_N + k))
        norm_root()
        act.wait_ge(mod_ready, 1)
        splits(KT_N, 0, lambda k: mod[:, k:k + 1])

        for tab in (COS, SIN):
            act.wait_ge(angle_ready, 1 if tab is COS else 2)
            act.activation(tab[:, :], tab[:, :], ACT.Sin).then_inc(rope_ready, 1)

        def step(m, func=ACT.Copy, scale=1.0, dst=None, waits=()):
            g = IN2 + m
            hi_next(g, g % 2, g // 2)
            act.wait_ge(slab_done, g + 2)
            for s, v in waits:
                act.wait_ge(s, v)
            act.activation(dst, Gf[g % 2], func, scale=scale).then_inc(psum_free[g % 2], 1)

        N_ROPED = 10
        for m in range(5):
            step(m, dst=T2[m % 2][:, :], waits=([(roped, m - 1)] if m >= 2 else []) + ([(wi_turned, 1)] if m == 2 else []))
        n = 0
        for i in range(TOPK_TILE, NT):
            for h in range(HEADS):
                act.wait_ge(idx_scores, n + 1)
                if n >= 2:
                    act.wait_ge(idx_added, n - 1)
                act.activation(T2[n % 2][:, 0:P * (i + 1)], Gf[n % 2][:, 0:P * (i + 1)], ACT.Relu,
                               scale=DH ** -0.5).then_inc(idx_relu, 1)
                n += 1
        act.wait_ge(idx_added, HEADS * NQ)
        for m in range(5, 11):
            step(m, dst=T2[m % 2][:, :], scale=-DH ** -0.5 if m < S_K else 1.0, waits=[(roped, m - 1)])
        for j in range(4):
            step(11 + 2 * j, dst=CU[:, j, PAD:PAD + S])
            step(12 + 2 * j, dst=SIG[:, :], func=ACT.Sigmoid, waits=[(glu_ready, j)] if j else [])
        attention(64, 128)
        turned_hi(0, 4, 20)
        for j in range(4):
            act.wait_ge(conv_centred, j + 1)
            act.wait_ge(sq_used, t_sqi.n - 1)
            t_sqi.inc(act.activation(SQ2[j % 2][:, :], YC[:, j, :], ACT.Square))
        norm_root()
        for j in range(4):
            t_hf.wait(act, 1)
            if j >= 2:
                act.wait_ge(x_split, 36 + j - 1)
            act.activation(HC[j % 2][:, :], YC[:, j, :], ACT.Silu, scale=V("conv_g", j),
                           bias=V("conv_nb", j)).then_inc(act_seq, 1)
            aseq.n += 1
            aseq.wait(act)
            act.activation(XH[:, 4 + j, :], HC[j % 2][:, :], ACT.Copy).then_inc(x_hi, 1)

        slabs_of(act, OUT2, 0, 8, only_hi)
        squares(lambda k: XT[:, k, :], lambda k: taken(OUT2 + k))
        norm_root()
        splits(KT_N, 0, lambda k: mod[:, 24 + k:25 + k])
        ffn(FFN2, 1)
        act.wait_ge(slab_done, 1 + SLABS)
        squares(lambda k: XT[:, k, :], lambda k: taken(SLABS - KT_N + k))
        norm_root()

    @block.tensor
    def _(pe):
        t_sq, t_stat = Tally(sq_used), Tally(stat_ready)
        t_diag, t_spread = Tally(diag_ready), Tally(spread_ready)

        def product(g, b, h, xh, xl, fresh=None, base=0):
            pe.wait_ge(lo_ready, g + 1)
            pe.wait_ge(psum_free[b], h + 1)
            for k in range(KT_N):
                if fresh is not None:
                    pe.wait_ge(fresh, base + k + 1)
                for n, (w, x) in enumerate(((whi, xh), (whi, xl), (wlo, xh))):
                    for half in range(2):
                        last = pe.matmul(G[b][:, half, :], w[b][:, k, :], x[:, k, half * HALF:(half + 1) * HALF],
                                         start=(k == 0 and n == 0), stop=(k == KT_N - 1 and n == 2))
            last.then_inc(slab_done, 1)

        def norm_stat(tiles, ssq):
            t_sq.wait(pe, tiles)
            for t in range(NT):
                last = pe.matmul(TP[1][:, 0, t:t + 1], ssq[:, t * P:(t + 1) * P], ones[:, 0:1], start=True, stop=True)
            t_stat.inc(last)

        def norm_spread(dg):
            t_diag.wait(pe, 1)
            for half in range(2):
                last = pe.matmul(TP[0][:, half, :], ones, dg[:, half * 4:half * 4 + 4, :].rearrange("p t n -> p (t n)"),
                                 start=True, stop=True)
            t_spread.inc(last)

        def norm(tiles=KT_N, ssq=SSQ, dg=DG):
            norm_stat(tiles, ssq)
            norm_spread(dg)

        pe.wait_ge(params_loaded, 32)
        pe.wait_ge(hot_loaded, 32)
        for c in range(4):
            last = pe.matmul(G[c // 2][0:HEADS, c % 2, :], RB[0:33, :], HOT[0:33, c * HALF:(c + 1) * HALF],
                             start=True, stop=True)
        last.then_inc(tab_made, 1)
        norm()
        pe.wait_ge(tab_copied, 1)

        x1 = lambda m, g, b, h: product(g, b, h, XH, XL)
        product(IN1, 0, 0, XH, XL, x_split, 0)
        slabs_of(pe, IN1, 1, 8, x1)

        def turn(b, h, n, par, waited=True):
            pe.wait_ge(psum_free[b], h + 2)
            if not (isinstance(n, int) and n < 2):
                pe.wait_ge(turn_out, n + (-1))
            for t in range(NT):
                last = pe.transpose(TP[par][:, t // 4, (t % 4) * P:(t % 4 + 1) * P], TT[b][:, t * P:(t + 1) * P], ident)
            last.then_inc(turned, 1)

        product(IN1 + 8, 0, 4, XH, XL)

        def with_turn(m, g, b, h):
            product(g, b, h, XH, XL)
            turn(1 - b, h + (0 if b else -1), m + (-9), 1 - b)

        slabs_of(pe, IN1, 9, 12, with_turn)
        slabs_of(pe, IN1, 12, 20, with_turn)
        turn(1, 9, 11, 1)

        pe.wait_ge(turn_out, 12)
        pe.wait_ge(sgu_loaded, 48)
        pe.wait_ge(mixed_ready, 1)
        for g in range(SGU_G):
            if g >= 2:
                pe.wait_ge(gated, g - 1)
            pe.matmul(TP[g % 2][:, 0, :], SGW[:, g, :], NAT[:, 2, :, g * DH:(g + 1) * DH],
                      start=True, stop=True).then_inc(mixed_mm, 1)
        pe.wait_ge(gated, SGU_G)

        def attention(n0, n1, ops):
            def scores(n):
                i, h, w = UNITS[n]
                q, k, _ = ops(i, h)
                if n >= n0 + 2:
                    pe.wait_ge(masked, n - 1)
                for c in range(0, w, 4):
                    cw = min(4, w - c) * P
                    last = pe.matmul(G[n % 2][:, c // 4, 0:cw], q, k[:, c * P:c * P + cw], start=True, stop=True)
                last.then_inc(scores_ready, 1)

            def turns(n):
                w = UNITS[n][2]
                pe.wait_ge(exped, n + 1)
                for half in range(2 if w > 4 else 1):
                    if half and n_b[n]:
                        pe.wait_ge(pt_b, n_b[n])
                    elif n:
                        pe.wait_ge(pt_a, n)
                    for c in range(4 * half, min(w, 4 * half + 4)):
                        last = pe.transpose(TP[0][:, half, (c % 4) * P:(c % 4 + 1) * P],
                                            PB[n % 3][:, c * P:(c + 1) * P], ident)
                    last.then_inc(half_turned, 1)

            def values(n):
                i, h, w = UNITS[n]
                v = ops(i, h)[2]
                pe.wait_ge(pt_a, n + 1)
                if w > 4:
                    pe.wait_ge(pt_b, n_b[n + 1])
                if n >= 2:
                    pe.wait_ge(att_out, n - 1)
                for c in range(w):
                    last = pe.matmul(TP[1][:, n % 2, 0:DH], PTS[n % 2][:, c * P:(c + 1) * P], v(c),
                                     start=(c == 0), stop=(c == w - 1))
                last.then_inc(pv_done, 1)

            for n in range(n0, n1 + 3):
                if n < n1:
                    scores(n)
                if n0 + 2 <= n < n1 + 2:
                    turns(n - 2)
                if n >= n0 + 3:
                    values(n - 3)

        def ops1(i, h):
            at_p = slice((h % 2) * DH, (h % 2 + 1) * DH)
            return (QT[at_p, h // 2, i * P:(i + 1) * P], KT[at_p, h // 2, :],
                    lambda c: NAT[:, 0, c, h * DH:(h + 1) * DH])

        attention(0, 64, ops1)

        def turn_mixed(src, n, base, xbase, flipped=0):
            for k in range(n):
                if k >= 2:
                    pe.wait_ge(x_split, xbase + k - 1)
                for t in range(NT):
                    dst = TP[(base + k) % 2][:, t // 4, (t % 4) * P:(t % 4 + 1) * P]
                    if k < flipped:
                        last = pe.matmul(dst, src(k, t), flip, start=True, stop=True)
                    else:
                        last = pe.transpose(dst, src(k, t), ident)
                last.then_inc(turned, 1)

        pe.wait_ge(att_out, 64)
        turn_mixed(lambda k, t: NATA[:, t, k * P:(k + 1) * P] if k < 4 else NAT[:, 1, t, (k - 4) * P:(k - 3) * P],
                   8, 12, 8, flipped=4)
        product(OUT1, OUT1 % 2, OUT1 // 2, XH, XL, x_split, 8)
        slabs_of(pe, OUT1, 1, 8, x1)
        norm()
        norm()

        def ffn(g0, which, xbase):
            with pe.Fori(0, GROUPS) as grp:
                for m in range(16):
                    g, b = g0 + m, (g0 + m) % 2
                    up = m < 8
                    product(grp * 16 + g, b, grp * 8 + g // 2, XH if up else UH, XL if up else UL,
                            *((x_split, xbase) if m == 0 else (u_split, grp * 8 + 32 * which) if m == 8 else ()))
                    if which == 0 and (up or m % 2):
                        a = m if up else 8 + (m - 8) // 2
                        pe.wait_ge(ada_red, grp * 12 + (a + 1))
                        pe.matmul(TP[1][:, 1, bass.ds(grp * 12 + a, 1)], RED[a % 2][:, :], ones[:, 0:1],
                                  start=True, stop=True).then_inc(mod_col, 1)

        ffn(FFN1, 0, 16)
        norm()
        norm()

        def swap_pairs(m):
            g = IN2 + m
            pe.wait_ge(psum_free[g % 2], g // 2 + 2)
            if m:
                pe.wait_ge(roped, m)
            for half in range(2):
                last = pe.matmul(TP[0][:, half, :], swap, T2[m % 2][:, half * HALF:(half + 1) * HALF],
                                 start=True, stop=True)
            last.then_inc(swapped, 1)

        for m in range(5):
            g = IN2 + m
            product(g, g % 2, g // 2, XH, XL, *((x_split, 24) if m == 0 else ()))
            if m:
                swap_pairs(m - 1)
            if m == 1:
                for t in range(NT):
                    last = pe.transpose(TP[1][:, 0, t * 8:t * 8 + 8], T2[0][DH:DH + 8, t * P:(t + 1) * P],
                                        ident[DH:DH + 8, DH:DH + 8])
                last.then_inc(wi_turned, 1)
        swap_pairs(4)
        pe.wait_ge(roped, 5)
        pe.wait_ge(ki_doubled, 16)
        n = 0
        for i in range(TOPK_TILE, NT):
            for h in range(HEADS):
                at_p = slice((h % 2) * DH, (h % 2 + 1) * DH)
                if n >= 2:
                    pe.wait_ge(idx_relu, n - 1)
                for c in range(0, i + 1, 4):
                    cw = min(4, i + 1 - c) * P
                    last = pe.matmul(G[n % 2][:, c // 4, 0:cw], QI[at_p, h // 2, i * P:(i + 1) * P],
                                     KI[at_p, c * P:c * P + cw], start=True, stop=True)
                last.then_inc(idx_scores, 1)
                n += 1
        pe.wait_ge(idx_relu, n)
        for m in range(5, 19):
            g = IN2 + m
            product(g, g % 2, g // 2, XH, XL)
            if 6 <= m <= 10:
                swap_pairs(m - 1)
            if m == 11:
                pe.wait_ge(psum_free[(g - 1) % 2], (g - 1) // 2 + 2)
                for t in range(NT):
                    last = pe.transpose(TP[1][:, t // 4, (t % 4) * P:(t % 4 + 1) * P], T2[0][:, t * P:(t + 1) * P], ident)
                last.then_inc(v2_turned, 1)

        def ops2(i, h):
            at_p = slice((h // 4) * DH, (h // 4 + 1) * DH)
            return (QT2[at_p, h % 4, i * P:(i + 1) * P], KT2[at_p, :],
                    lambda c: V2[:, c, (h // 4) * DH:(h // 4 + 1) * DH])

        pe.wait_ge(roped, 10)
        pe.wait_ge(v2_ready, 1)
        pe.wait_ge(glu_ready, 4)
        attention(64, 128, ops2)
        pe.wait_ge(att_out, 128)
        turn_mixed(lambda k, t: NATA[:, t, k * P:(k + 1) * P], 4, 20, 32)
        pe.wait_ge(x_split, 36)
        pe.wait_ge(conv_ready, 4)
        for half in range(2):
            for j in range(4):
                last = pe.matmul(TP[1][:, half, :], ones, YC[:, j, half * HALF:(half + 1) * HALF],
                                 start=(j == 0), stop=(j == 3))
        last.then_inc(conv_mean, 1)
        norm(4, SSQ2, DG2)
        product(OUT2, OUT2 % 2, OUT2 // 2, XH, XL, x_split, 32)
        slabs_of(pe, OUT2, 1, 8, x1)
        norm()
        ffn(FFN2, 1, 40)
        norm()

    @block.vector
    def _(dve):
        d = Tally(dve_seq)
        t_sq, t_squ = Tally(sq_ready), Tally(sq_used)
        t_stat, t_var, t_root = Tally(stat_ready), Tally(var_ready), Tally(root_ready)
        t_diag, t_spread, t_hf = Tally(diag_ready), Tally(spread_ready), Tally(hf_ready)
        t_xt = Tally(xt_ready)

        def seq(ins):
            d.inc(ins)
            d.wait(dve)

        dve.memset(RB[0:33, :], 1.0).then_inc(cleared, 1)
        for n, s in enumerate((slab_done, psum_free[0], psum_free[1], usq_ready, mod_col, mod_col)):
            dve.memset(keep[:, n:n + 1], 0).then_inc(s, 1)

        def lo(g, b):
            dve.wait_ge(hi_ready, g + 1)
            dve.tensor_tensor(wlo[b][:, :, :].rearrange("p k n -> p (k n)"), raw[b][:, :],
                              whi[b][:, :, :].bitcast(F32).rearrange("p k n -> p (k n)"), ALU.subtract).then_inc(lo_ready, 1)

        def sum_squares(tiles=KT_N, sq=SQ, ssq=SSQ):
            for k in range(tiles):
                t_sq.wait(dve, 1)
                if k == 0:
                    t_squ.inc(dve.tensor_copy(ssq[:, :], sq[0][:, :]))
                else:
                    t_squ.wait(dve)
                    t_squ.inc(dve.tensor_tensor(ssq[:, :], ssq[:, :], sq[k % 2][:, :], ALU.add))

        def reciprocal_root():
            t_root.wait(dve, 1)
            seq(dve.reciprocal(y0[:, :], root[:, :]))
            seq(dve.tensor_tensor(aa[:, :], y0[:, :], y0[:, :], ALU.mult))
            seq(dve.tensor_tensor(aa[:, :], aa[:, :], var[:, :], ALU.mult))
            seq(dve.tensor_scalar(aa[:, :], aa[:, :], -0.5, 1.5, ALU.mult, ALU.add))
            seq(dve.tensor_tensor(rstd[:, :], y0[:, :], aa[:, :], ALU.mult))

        def norm(width, eps, tiles=KT_N, sq=SQ, ssq=SSQ, dg=DG):
            sum_squares(tiles, sq, ssq)
            t_stat.wait(dve, 1)
            t_var.inc(dve.tensor_scalar(var[:, :], TP[1][:, 0, 0:NT], 1.0 / width, eps, ALU.mult, ALU.add))
            t_var.wait(dve)
            reciprocal_root()
            t_diag.inc(dve.tensor_tensor(dg[:, :, :], ident.unsqueeze(1).broadcast_to([P, NT, P]),
                                         rstd[:, :].unsqueeze(2).broadcast_to([P, NT, P]), ALU.mult))
            t_spread.wait(dve, 1)

        def split_norm(scale, bias, base):
            def low(k):
                dve.wait_ge(x_hi, base + k + 1)
                hi_part = XH[:, k, :].bitcast(F32)
                if bias is None:
                    dve.tensor_tensor(XL[:, k, :], HF[k % 2][:, :], hi_part, ALU.subtract).then_inc(x_split, 1)
                else:
                    dve.scalar_tensor_tensor(out=XL[:, k, :], in0=HF[k % 2][:, :], scalar=bias(k), in1=hi_part,
                                             op0=ALU.add, op1=ALU.subtract).then_inc(x_split, 1)

            for k in range(KT_N):
                if k >= 2:
                    dve.wait_ge(x_split, base + k - 1)
                t_hf.inc(dve.scalar_tensor_tensor(out=HF[k % 2][:, :], in0=XT[:, k, :], scalar=scale(k), in1=TPf[0],
                                                  op0=ALU.mult, op1=ALU.mult))
                if k:
                    low(k - 1)
            t_hf.wait(dve)
            low(KT_N - 1)

        def residual(src, gain, n0):
            for k in range(KT_N):
                seq(dve.scalar_tensor_tensor(out=src[:, k, :], in0=src[:, k, :], scalar=gain(k), in1=TPf[0],
                                             op0=ALU.mult, op1=ALU.mult))
                dve.wait_ge(xre_loaded[k % 4], 16 * (n0 + k // 4 + 1))
                t_xt.inc(dve.tensor_tensor(XT[:, k, :], src[:, k, :], XRE[:, k % 4, :], ALU.add))

        dve.wait_ge(tab_made, 1)
        for b in range(2):
            last = dve.tensor_scalar(TAB[0:HEADS, b * S:(b + 1) * S], Gf[b][0:HEADS, :], -1.0, None, ALU.mult)
        last.then_inc(tab_copied, 1)
        lo(0, 0)
        norm(D, RMS_EPS)
        dve.wait_ge(tab_stored, 16)
        split_norm(lambda k: V("g_pre_mix", k), None, 0)

        def only_lo(m, g, b, h):
            lo(g + 1, 1 - b)

        slabs_of(dve, IN1, 0, 8, only_lo)
        def turned_tile(n):
            dve.wait_ge(turned, n + 1)
            dve.tensor_copy(NAT[:, n // 4, :, (n % 4) * P:(n % 4 + 1) * P],
                            TPf[n % 2].rearrange("p (t c) -> p t c", t=NT)).then_inc(turn_out, 1)

        for m in range(8, 20):
            lo(IN1 + m + 1, (m + 1) % 2)
            if m >= 10:
                turned_tile(m - 10)
        turned_tile(10)
        turned_tile(11)

        dve.wait_ge(turn_out, 12)
        for t in range(NT):
            seq(dve.bn_stats(bn6[:, 6 * t:6 * t + 6], NAT[:, 2, t, :]))
            last = dve.bn_aggr(mv[:, 2 * t:2 * t + 2], bn6[:, 6 * t:6 * t + 6])
        seq(last)
        mv3 = mv[:, :].rearrange("p (t c) -> p t c", c=2)
        t_var.inc(dve.tensor_scalar(var[:, :], mv3[:, :, 1], SGU_EPS, None, ALU.add))
        t_var.wait(dve)
        reciprocal_root()
        for t in range(NT):
            last = dve.tensor_scalar(NAT[:, 2, t, :], NAT[:, 2, t, :], mv3[:, t, 0:1], rstd[:, t:t + 1],
                                     ALU.subtract, ALU.mult)
        seq(last)
        dve.wait_ge(sgu_loaded, 48)
        for r, op in ((0, ALU.mult), (1, ALU.add)):
            last = dve.tensor_tensor(NAT[:, 2, :, :], NAT[:, 2, :, :],
                                     LNG[:, r, :].unsqueeze(1).broadcast_to([P, NT, ATT]), op)
            if r == 0:
                seq(last)
        last.then_inc(mixed_ready, 1)
        for g in range(SGU_G):
            dve.wait_ge(mixed_mm, g + 1)
            z = NAT[:, 1, :, g * DH:(g + 1) * DH]
            dve.scalar_tensor_tensor(out=z, in0=TP[g % 2][:, 0, :].rearrange("p (n c) -> p n c", n=NT),
                                     scalar=V("sgu_b", g), in1=z, op0=ALU.add, op1=ALU.mult).then_inc(gated, 1)

        def attention(n0, n1, bias_of, meanwhile=None):
            def mask(n):
                i, h, w = UNITS[n]
                bias = bias_of(n)
                dve.wait_ge(scores_ready, n + 1)
                if n >= 3:
                    dve.wait_ge(half_turned, n_half[n - 2])
                dve.tensor_tensor_reduce(out=PB[n % 3][:, 0:w * P], in0=Gf[n % 2][:, 0:w * P], in1=bias, scale=1.0,
                                         scalar=HIGHEST, op0=ALU.add, op1=ALU.min,
                                         accum_out=negm[:, n % 3:n % 3 + 1]).then_inc(masked, 1)

            def copy_b(n):
                w = (UNITS[n][2] - 4) * P
                if w > 0:
                    dve.wait_ge(half_turned, n_half[n + 1])
                    if n >= 2:
                        dve.wait_ge(pv_done, n - 1)
                    dve.tensor_copy(PTS[n % 2][:, 4 * P:4 * P + w], TPf[0][:, 4 * P:4 * P + w]).then_inc(pt_b, 1)

            def out(n):
                i, h, _ = UNITS[n]
                dve.wait_ge(pv_done, n + 1)
                seq(dve.reciprocal(rden[:, n % 2:n % 2 + 1], den[:, n % 4:n % 4 + 1]))
                dve.tensor_scalar(NATA[:, i, h * DH:(h + 1) * DH], TP[1][:, n % 2, 0:DH], rden[:, n % 2:n % 2 + 1], None,
                                  ALU.mult).then_inc(att_out, 1)

            for n in range(n0, n1 + 3):
                if n < n1:
                    mask(n)
                if n0 + 2 <= n < n1 + 2:
                    copy_b(n - 2)
                if n >= n0 + 3:
                    out(n - 3)
                if meanwhile:
                    meanwhile(n - n0)

        def bias1(n):
            i, h, _ = UNITS[n]
            if i == 0:
                dve.wait_ge(bias_loaded[h % 2], 16 * (h // 2 + 1))
            return BIAS[h % 2][:, 896 - i * P:896 - i * P + S]

        attention(0, 64, bias1)

        def turned_lo(n, base, xbase):
            for k in range(n):
                dve.wait_ge(turned, base + k + 1)
                dve.wait_ge(x_hi, xbase + k + 1)
                dve.tensor_tensor(XL[:, k, :], TPf[(base + k) % 2], XH[:, k, :].bitcast(F32),
                                  ALU.subtract).then_inc(x_split, 1)

        turned_lo(8, 12, 8)

        def out1(m, g, b, h):
            lo(g + 1, 1 - b)
            dve.wait_ge(slab_done, g + 2)
            dst = ACC[:, bass.ds(m, 1), :].rearrange("p a t -> p (a t)") if not isinstance(m, int) else ACC[:, m, :]
            dve.tensor_copy(dst, Gf[b]).then_inc(psum_free[b], 1)

        slabs_of(dve, OUT1, 0, 8, out1)
        norm(D, RMS_EPS)
        residual(ACC, lambda k: V("g_post_mix", k), 0)
        norm(D, RMS_EPS)
        split_norm(lambda k: V("g_pre_ffn", k), None, 16)
        dve.wait_ge(spilled, 16)
        for k in range(KT_N):
            last = dve.memset(XT[:, k, :], 0.0)
        seq(last)

        def ffn(g0, which, scale):
            with dve.Fori(0, GROUPS) as grp:
                for m in range(16):
                    g, b = g0 + m, (g0 + m) % 2
                    lo(grp * 16 + (g + 1), 1 - b)
                    if which == 0 and (m < 8 or m % 2):
                        a = m if m < 8 else 8 + (m - 8) // 2
                        dve.wait_ge(ada_prod, grp * 12 + (a + 1))
                        dve.wait_ge(mod_col, grp * 12 + (a + 1))
                        dve.tensor_reduce(RED[a % 2][:, :], ADA[a % 2][:, :, :].rearrange("p k n -> p n k"), AX.X,
                                          ALU.add).then_inc(ada_red, 1)
                    if m < 8:
                        u = grp * 8 + (32 * which + m)
                        dve.wait_ge(psum_free[b], grp * 8 + (g // 2 + 2))
                        if m:
                            dve.wait_ge(u_split, u)
                        dve.tensor_tensor(USQ[:, :], RELU[:, :], RELU[:, :], ALU.mult).then_inc(usq_ready, 1)
                        dve.wait_ge(usq_ready, u + 2)
                        dve.wait_ge(u_hi, u + 1)
                        dve.tensor_tensor(UL[:, m, :], USQ[:, :], UH[:, m, :].bitcast(F32), ALU.subtract).then_inc(u_split, 1)
                    else:
                        dve.wait_ge(slab_done, grp * 16 + (g + 2))
                        dve.scalar_tensor_tensor(out=XT[:, m - 8, :], in0=Gf[b], scalar=scale(m - 8), in1=XT[:, m - 8, :],
                                                 op0=ALU.mult, op1=ALU.add).then_inc(psum_free[b], 1)

        ffn(FFN1, 0, lambda k: 1.0)
        dve.wait_ge(mod_col, 50)
        seq(dve.tensor_tensor(mod[:, :], TP[1][:, 1, 0:48], vec[:, VCOL["b_ada"]:VCOL["b_ada"] + 48], ALU.add))
        for r, name in enumerate(("g_mix", "g_mlp")):
            last = dve.scalar_tensor_tensor(out=scl[:, 8 * r:8 * r + 8], in0=mod[:, 24 * r + 8:24 * r + 16], scalar=1.0,
                                            in1=vec[:, VCOL[name]:VCOL[name] + 8], op0=ALU.add, op1=ALU.mult)
        last.then_inc(mod_ready, 1)
        norm(D, RMS_EPS)
        residual(XT, lambda k: V("g_post_ffn", k), 2)
        norm(D, RMS_EPS)
        dve.wait_ge(mod_ready, 1)
        split_norm(lambda k: scl[:, k:k + 1], lambda k: mod[:, k:k + 1], 24)

        dve.wait_ge(pos_loaded, 16)
        seq(dve.tensor_scalar(T1[:, :], POSI[:, :], freq, None, ALU.mult))
        MAGIC = 1.5 * 2.0 ** 23
        C1 = 6.28125
        C2 = float(np.float32(round((2 * np.pi - C1) * 2 ** 21) / 2 ** 21))
        C3 = float(2 * np.pi - C1 - C2)
        for tab, quarter in ((COS, 0.25), (SIN, 0.0)):
            seq(dve.tensor_scalar(TK2[:, :], T1[:, :], float(1 / (2 * np.pi)), quarter, ALU.mult, ALU.add))
            seq(dve.tensor_scalar(TK2[:, :], TK2[:, :], MAGIC, MAGIC, ALU.add, ALU.subtract))
            src = T1
            for c in (C1, C2, C3):
                seq(dve.scalar_tensor_tensor(out=tab[:, :], in0=TK2[:, :], scalar=-c, in1=src[:, :], op0=ALU.mult,
                                             op1=ALU.add))
                src = tab
            seq(dve.tensor_scalar(tab[:, :], tab[:, :], float(2 * np.pi * quarter), 3.1415925, ALU.add, ALU.min))
            dve.tensor_scalar(tab[:, :], tab[:, :], -3.1415925, None, ALU.max).then_inc(angle_ready, 1)

        lo(IN2 + 1, (IN2 + 1) % 2)

        def rope(m, dst):
            if m == 0:
                dve.wait_ge(rope_ready, 2)
            dve.wait_ge(swapped, m + 1)
            dve.tensor_tensor(T1[:, :], T2[m % 2][:, :], COS[:, :], ALU.mult)
            seq(dve.tensor_tensor(dst, TPf[0], SIN[:, :], ALU.mult))
            dve.tensor_tensor(dst, dst, T1[:, :], ALU.add).then_inc(roped, 1)

        for m in range(1, 5):
            lo(IN2 + m + 1, (IN2 + m + 1) % 2)
            rope(m - 1, KI[:, :] if m == 1 else QI[:, m - 2, :])
            if m == 1:
                dve.wait_ge(wi_turned, 1)
                seq(dve.tensor_scalar(wi[:, :], TP[1][:, 0, 0:8 * NT], float(np.float32(HEADS ** -0.5)), None, ALU.mult))
        rope(4, QI[:, 3, :])
        n = 0
        for i in range(TOPK_TILE, NT):
            sc = SC[:, score_at(i):score_at(i + 1)]
            for h in range(HEADS):
                w = wi[:, 8 * i + h:8 * i + h + 1]
                dve.wait_ge(idx_relu, n + 1)
                r = T2[n % 2][:, 0:P * (i + 1)]
                if h == 0:
                    dve.tensor_scalar(sc, r, w, None, ALU.mult).then_inc(idx_added, 1)
                else:
                    dve.wait_ge(idx_added, n)
                    dve.scalar_tensor_tensor(out=sc, in0=r, scalar=w, in1=sc, op0=ALU.mult, op1=ALU.add).then_inc(idx_added, 1)
                n += 1

        tiles = [(n, i, SC[:, score_at(i):score_at(i + 1)]) for n, i in enumerate(range(TOPK_TILE, NT))]

        def count(op, level):
            for n, i, sc in tiles:
                if n >= 2:
                    dve.wait_ge(dve_seq, d.n - 1)
                d.inc(dve.tensor_scalar(JUNK[:, n % 2, 0:P * (i + 1)], sc, level(n), None, op, ALU.add,
                                        accum_out=cnt[:, n:n + 1]))
            d.wait(dve)

        def select_sign():
            dve.wait_ge(idx_masked, NQ)
            count(ALU.is_ge, lambda n: 0.0)
            seq(dve.tensor_scalar(sgn[:, :], cnt[:, :], float(TOPK), None, ALU.is_ge))
            for n, i, sc in tiles:
                below = P * (i + 1) - TOPK + 1
                last = dve.tensor_scalar(need[:, n:n + 1], sgn[:, n:n + 1], float(TOPK - below), float(below),
                                         ALU.mult, ALU.add)
            seq(last)
            dve.memset(mag[:, :], 0)
            seq(dve.tensor_scalar(sgn[:, :], sgn[:, :], 2.0, -1.0, ALU.mult, ALU.add))
            for n, i, sc in tiles:
                last = dve.tensor_scalar(sc, sc, sgn[:, n:n + 1], None, ALU.mult)
            seq(last)

        def select_bit(bit):
            seq(dve.tensor_scalar(cand[:, :], mag[:, :], 1 << bit, None, ALU.bitwise_or))
            count(ALU.is_ge, lambda n: cand[:, n:n + 1].bitcast(F32))
            seq(dve.tensor_tensor(keep[:, :], cnt[:, :], need[:, :], ALU.is_ge))
            seq(dve.copy_predicated(mag[:, :], keep[:, :], cand[:, :]))

        def select_masks():
            seq(dve.tensor_tensor(thr[:, :], mag[:, :].bitcast(F32), sgn[:, :], ALU.mult))
            for n, i, sc in tiles:
                w = P * (i + 1)
                above, equal, rank = TK1[:, 0:w], TK2[:, 0:w], T1[:, 0:w]
                seq(dve.tensor_scalar(sc, sc, sgn[:, n:n + 1], None, ALU.mult))
                dve.tensor_scalar(equal, sc, thr[:, n:n + 1], None, ALU.is_equal)
                seq(dve.tensor_scalar(above, sc, thr[:, n:n + 1], None, ALU.is_gt, ALU.add, accum_out=cnt[:, n:n + 1]))
                seq(dve.tensor_scalar(need[:, n:n + 1], cnt[:, n:n + 1], -1.0, float(TOPK), ALU.mult, ALU.add))
                seq(dve.tensor_tensor_scan(rank, equal, equal, 0.0, ALU.add, ALU.max))
                seq(dve.scalar_tensor_tensor(out=equal, in0=rank, scalar=need[:, n:n + 1], in1=equal, op0=ALU.is_le,
                                             op1=ALU.mult))
                seq(dve.scalar_tensor_tensor(out=sc, in0=equal, scalar=-1.0, in1=above, op0=ALU.add, op1=ALU.add))
                seq(dve.tensor_scalar(sc, sc, FAR, None, ALU.mult))

        bits = list(range(BITS - 1, -1, -1))
        select_sign()
        for m in range(5, 19):
            lo(IN2 + m + 1, (IN2 + m + 1) % 2)
            if 6 <= m <= 10:
                rope(m - 1, QT2[:, m - 6, :] if m < 10 else KT2[:, :])
            if m == 11:
                dve.wait_ge(v2_turned, 1)
                dve.tensor_copy(V2[:, :, :].rearrange("p t c -> p (t c)"), TPf[1]).then_inc(v2_ready, 1)
            if m >= 13 and m % 2 == 1:
                j = (m - 13) // 2
                g = IN2 + m - 1
                dve.wait_ge(psum_free[g % 2], g // 2 + 2)
                dve.tensor_tensor(CU[:, j, PAD:PAD + S], CU[:, j, PAD:PAD + S], SIG[:, :], ALU.mult).then_inc(glu_ready, 1)
            for _ in range(3 if m < 8 else 2):
                if bits:
                    select_bit(bits.pop(0))
        g = IN2 + 18
        dve.wait_ge(psum_free[g % 2], g // 2 + 2)
        dve.tensor_tensor(CU[:, 3, PAD:PAD + S], CU[:, 3, PAD:PAD + S], SIG[:, :], ALU.mult).then_inc(glu_ready, 1)
        while bits:
            select_bit(bits.pop(0))
        select_masks()

        dve.wait_ge(glu_ready, 4)
        dve.wait_ge(pool_seq, 2)
        conv0 = d.n
        taps = [(tap, j) for tap in range(CONV_K) for j in range(4)]
        done = {}

        def conv(step):
            for tap, j in taps[2 * step:2 * step + 2]:
                w = V("conv_w", j * CONV_K + tap)
                src = CU[:, j, tap:tap + S]
                if tap == 0:
                    ins = dve.tensor_scalar(YC[:, j, :], src, w, V("conv_b", j), ALU.mult, ALU.add)
                else:
                    dve.wait_ge(dve_seq, done[j])
                    ins = dve.scalar_tensor_tensor(out=YC[:, j, :], in0=src, scalar=w, in1=YC[:, j, :], op0=ALU.mult,
                                                   op1=ALU.add)
                if tap == CONV_K - 1:
                    ins.then_inc(conv_ready, 1)
                else:
                    d.inc(ins)
                    done[j] = d.n

        def bias2(n):
            i = UNITS[n][0]
            if i >= TOPK_TILE:
                return SC[:, score_at(i):score_at(i + 1)]
            if n == 64:
                dve.wait_ge(mask01, 2)
            return MASK01[:, 0:P] if i == 0 else MASK01[:, P:3 * P]

        attention(64, 128, bias2, conv)
        turned_lo(4, 20, 32)
        dve.wait_ge(conv_mean, 1)
        for j in range(4):
            dve.scalar_tensor_tensor(out=YC[:, j, :], in0=TPf[1], scalar=-1.0 / ATT, in1=YC[:, j, :], op0=ALU.mult,
                                     op1=ALU.add).then_inc(conv_centred, 1)
        norm(ATT, RMS_EPS, 4, SQ2, SSQ2, DG2)
        for j in range(4):
            t_hf.inc(dve.tensor_tensor(YC[:, j, :], YC[:, j, :], TPf[0], ALU.mult))
        for j in range(4):
            dve.wait_ge(x_hi, 36 + j + 1)
            dve.tensor_tensor(XL[:, 4 + j, :], HC[j % 2][:, :], XH[:, 4 + j, :].bitcast(F32), ALU.subtract).then_inc(x_split, 1)

        dve.wait_ge(x_back, 16)
        for m in range(8):
            g = OUT2 + m
            lo(g + 1, (g + 1) % 2)
            dve.wait_ge(slab_done, g + 2)
            dve.scalar_tensor_tensor(out=XT[:, m, :], in0=Gf[g % 2], scalar=mod[:, 16 + m:17 + m], in1=XT[:, m, :],
                                     op0=ALU.mult, op1=ALU.add).then_inc(psum_free[g % 2], 1)
        norm(D, RMS_EPS)
        split_norm(lambda k: scl[:, 8 + k:9 + k], lambda k: mod[:, 24 + k:25 + k], 40)
        ffn(FFN2, 1, lambda k: mod[:, 40 + k:41 + k])
        norm(D, RMS_EPS)
        for k in range(KT_N):
            t_hf.inc(dve.scalar_tensor_tensor(out=XT[:, k, :], in0=XT[:, k, :], scalar=V("g_final", k), in1=TPf[0],
                                              op0=ALU.mult, op1=ALU.mult))

    return ctx


def in_slabs(w, cols=None):
    if cols is not None:
        w = np.concatenate([w[:, c:c + n] for c, n in cols], axis=1)
    m = w.shape[1] // P
    return w.reshape(KT_N, P, m, P).transpose(2, 1, 0, 3).reshape(m, P, S)


def columns(v):
    return np.asarray(v).reshape(-1, P).T


def kernel(**inputs):
    import concourse.bacc as bacc
    from concourse.bass_utils import run_bass_kernel_spmd

    a = {k: np.asarray(v) for k, v in inputs.items()}
    w_in2 = a["w_in_2"][0]
    one, pair = P, DH
    heads = [(h * DH + 4 * DH * r, pair) for h in range(4) for r in range(2)]
    in2 = ([(1280, one)] + [(768 + one * m, one) for m in range(4)] + heads + [(512, one), (640, one)]
           + [(1352 + ATT * r + one * j, one) for j in range(4) for r in range(2)])

    def feed_forward(w1, w2):
        parts = []
        for g in range(GROUPS):
            parts += [in_slabs(w1[:, g * D:(g + 1) * D]), in_slabs(w2[g * D:(g + 1) * D, :])]
        return parts

    w_in1 = a["w_in"][0]
    slabs = np.concatenate(
        [in_slabs(w_in1), in_slabs(a["w_out"][0])] + feed_forward(a["w_ff1"][0], a["w_ff2"][0])
        + [in_slabs(w_in2, in2), in_slabs(a["w_out_2"][0])] + feed_forward(a["w_up_2"][0], a["w_down_2"][0])
        + [in_slabs(w_in1[:, 0:P])])
    packed = {
        "g_pre_mix": columns(a["g_pre_mix"]), "g_post_mix": columns(a["g_post_mix"]),
        "g_pre_ffn": columns(a["g_pre_ffn"]), "g_post_ffn": columns(a["g_post_ffn"]), "sgu_b": a["sgu_b"][0].T,
        "b_ada": columns(a["b_ada_2"]), "g_mix": columns(a["g_mix_2"]),
        "conv_w": a["conv_w_2"][0].reshape(CONV_K, 4, P).transpose(2, 1, 0).reshape(P, 4 * CONV_K),
        "conv_b": columns(a["conv_b_2"]), "conv_g": columns(a["conv_norm_g_2"]), "conv_nb": columns(a["conv_norm_b_2"]),
        "g_mlp": columns(a["g_mlp_2"]), "g_final": columns(a["g_final_2"]), "c": columns(a["c_2"]),
    }
    consts = np.zeros((P, N_CONST), np.float32)
    consts[:, 0:P] = np.eye(P)
    for base in range(0, P, DH):
        for r in range(8):
            consts[base + 8 + r, P + base + r] = -1.0
            consts[base + r, P + base + 8 + r] = 1.0
            f = np.power(np.float32(500000.0), np.float32(-r * 2.0 / 16))
            consts[base + r, 4 * P] = consts[base + 8 + r, 4 * P] = f
    consts[:, 2 * P:3 * P] = 1.0
    consts[:, 3 * P:4 * P] = np.eye(P)[::-1]
    arrays = {
        "slabs": slabs, "ada": in_slabs(a["w_ada_2"][0]), "xT": a["x"][0].T,
        "vecs": np.concatenate([packed[name] for name, _ in VECS], axis=1),
        "lnrow": np.concatenate([a["sgu_ln_g"], a["sgu_ln_b"]]),
        "sgu_wT": a["sgu_w"][0].transpose(2, 0, 1).reshape(P, SGU_G * P),
        "rel_bias": a["rel_bias"], "positions": a["positions_2"], "consts": consts, "hot": t5_tables(),
    }
    nc = bacc.Bacc("TRN2", target_bir_lowering=False, num_devices=1)
    args = []
    for name in arrays:
        arrays[name] = np.ascontiguousarray(arrays[name])
        args.append(nc.dram_tensor(name, arrays[name].shape, mybir.dt.from_np(arrays[name].dtype), kind="ExternalInput").ap())
    args.append(nc.dram_tensor("outT", (D, S), F32, kind="ExternalOutput").ap())
    with build(nc, *args):
        pass
    r = run_bass_kernel_spmd(nc, [arrays], core_ids=[0])
    return np.ascontiguousarray(r.results[0]["outT"].T).reshape(1, S, D)
```

```python
from contextlib import ExitStack

import numpy as np

import concourse.bass as bass
from concourse import mybir

F32 = mybir.dt.float32
F32R = mybir.dt.float32r
U32 = mybir.dt.uint32
U8 = mybir.dt.uint8
I32 = mybir.dt.int32
ACT = mybir.ActivationFunctionType
ALU = mybir.AluOpType
AX = mybir.AxisListType

P = 128
S = 1024
D = 1024
KT_N = D // P
HALF = 512
NT = S // P
DH = 64
HEADS = 8
ATT = HEADS * DH
D_FF = 4 * D
GROUPS = D_FF // D
TOPK = 256
TOPK_TILE = TOPK // P
CONV_K = 31
PAD = CONV_K - 1
SGU_G = 8
FAR = -1e30
HIGHEST = 3.4028234e38
LOWEST = -HIGHEST
RMS_EPS = 1e-6
SGU_EPS = 1e-5
BITS = 31

IN1, N_IN1 = 0, 20
OUT1 = IN1 + N_IN1
FFN1 = OUT1 + 8
IN2, N_IN2 = FFN1 + 16 * GROUPS, 19
OUT2 = IN2 + N_IN2
FFN2 = OUT2 + 8
SLABS = FFN2 + 16 * GROUPS
STREAM = SLABS + 1
S_ZU, S_ZV, S_Q1, S_K1, S_V1 = 0, 4, 8, 12, 16
S_KI, S_QI, S_Q, S_K, S_V, S_CONV = 0, 1, 5, 9, 10, 11

VECS = [("g_pre_mix", 8), ("g_post_mix", 8), ("g_pre_ffn", 8), ("g_post_ffn", 8), ("sgu_b", 8), ("b_ada", 48),
        ("g_mix", 8), ("conv_w", 4 * CONV_K), ("conv_b", 4), ("conv_g", 4), ("conv_nb", 4), ("g_mlp", 8),
        ("g_final", 8), ("c", 8)]
VCOL, _n = {}, 0
for _name, _k in VECS:
    VCOL[_name] = _n
    _n += _k
N_VEC = _n

A_VEC = 16544
A_CONST = A_VEC + 4 * N_VEC
N_CONST = 4 * P + 1
A_SMALL = A_CONST + 4 * N_CONST + 28
A_RAW = A_SMALL + 2560
A_WHI = A_RAW + 8192
A_WLO = A_WHI + 8192
A_XT = A_WLO + 8192
A_XH = A_XT + 32768
A_XL = A_XH + 32768
A_R = A_XL + 32768
N_SCORE = sum(P * (i + 1) for i in range(TOPK_TILE, NT))


def score_at(i):
    return sum(P * (j + 1) for j in range(TOPK_TILE, i))


def t5_tables():
    n_rel = 2 * S
    hot = np.zeros((33, n_rel), np.float32)
    for col in range(n_rel):
        rel = col - S
        n = abs(rel)
        if n < 8:
            bucket = n
        else:
            bucket = min(8 + int(np.floor(np.log(n / 8) / np.log(1024 / 8) * 8)), 15)
        if rel > 0:
            bucket += 16
        hot[bucket, col] = 1.0
        seen = (n <= 64) + (n % 4 == 0 and n <= 256) + (n % 16 == 0 and n <= 1024)
        hot[32, col] = np.log(seen) if seen else FAR
    return hot


class Tally:

    def __init__(self, sem, n=0):
        self.sem, self.n = sem, n

    def inc(self, ins):
        self.n += 1
        ins.then_inc(self.sem, 1)

    def wait(self, eng, by=0):
        self.n += by
        if self.n > 0:
            eng.wait_ge(self.sem, self.n)


def build(nc, slabs, ada, xT, vecs, lnrow, sgu_wT, rel_bias, positions, consts, hot, outT, dbg=None):
    ctx = ExitStack()

    def at(name, shape, off, dt=F32):
        return nc.alloc_sbuf_tensor_at(name, shape, dt, offset=off)

    def sem(name):
        return ctx.enter_context(nc.semaphore(name))

    vec = at("vec", [P, N_VEC], A_VEC)
    cst = at("cst", [P, N_CONST], A_CONST)
    ident, swap, ones, flip = (cst[:, n * P:(n + 1) * P] for n in range(4))
    freq = cst[:, 4 * P:4 * P + 1]

    small_at = [A_SMALL]

    def small(name, n, dt=F32):
        t = at(name, [P, n], small_at[0], dt)
        small_at[0] += -(-4 * n // 32) * 32
        assert small_at[0] <= A_RAW
        return t

    raw = [at(f"raw{b}", [P, S], A_RAW + 4096 * b) for b in range(2)]
    whi = [at(f"whi{b}", [P, KT_N, P], A_WHI + 4096 * b, F32R) for b in range(2)]
    wlo = [at(f"wlo{b}", [P, KT_N, P], A_WLO + 4096 * b, F32R) for b in range(2)]
    XT = at("XT", [P, KT_N, S], A_XT)
    XH = at("XH", [P, KT_N, S], A_XH, F32R)
    XL = at("XL", [P, KT_N, S], A_XL, F32R)

    NORM0 = A_R + 32768
    SQ = [at(f"SQ{b}", [P, S], NORM0 + 4096 * b) for b in range(2)]
    SSQ = at("SSQ", [P, S], NORM0 + 8192)
    DG = at("DG", [P, NT, P], NORM0 + 12288)
    HF = [at(f"HF{b}", [P, S], NORM0 + 16384 + 4096 * b) for b in range(2)]
    XRE = at("XRE", [P, 4, S], NORM0 + 24576)
    SQF = [at(f"SQF{b}", [P, S], A_XL + 4096 * b) for b in range(2)]
    SSQF = at("SSQF", [P, S], A_XL + 8192)
    DGF = at("DGF", [P, NT, P], A_XL + 12288)
    ACC = at("ACC", [P, KT_N, S], A_R)

    QT = at("QT", [P, 4, S], A_R)
    KT = at("KT", [P, 4, S], A_R + 16384)
    NAT = at("NAT", [P, 3, NT, ATT], A_R + 32768)
    TT = [at(f"TT{b}", [P, S], A_XT + 4096 * b) for b in range(2)]
    BIAS = [at(f"BIAS{b}", [P, 1920], A_XT + 8192 + 7680 * b) for b in range(2)]
    TAB = at("TAB", [P, 2 * S], A_XL + 0)
    HOT = at("HOT", [P, 2 * S], A_XL + 8192)
    LNG = at("LNG", [P, 2, ATT], A_XT + 23552)
    SGW = at("SGW", [P, SGU_G, P], A_XT + 27648)
    A_GATE = A_R + 49152
    QS = [at(f"QS{b}", [P, S], o, F32R) for b, o in enumerate((A_XT + 23552, A_GATE))]
    KS = [at(f"KS{b}", [P, S], o, F32R) for b, o in enumerate((A_XT + 27648, A_GATE + 4096))]
    KL = at("KL", [P, S], A_GATE + 8192, F32R)
    PB = [at(f"PB{b}", [P, S], A_XH + 4096 * b) for b in range(3)]
    PTS = [at(f"PTS{b}", [P, S], A_XH + 24576 + 4096 * b) for b in range(2)]
    NATA = at("NATA", [P, NT, ATT], A_XL + 16384)
    UH = at("UH", [P, KT_N, S], A_R, F32R)
    UL = at("UL", [P, KT_N, S], A_R + 32768, F32R)
    RELU = at("RELU", [P, S], A_R + 65536)
    USQ = at("USQ", [P, S], A_R + 65536 + 4096)
    RBS = at("RBS", [P, S], A_R + 65536 + 4096)
    ADA = [at(f"ADA{b}", [P, KT_N, P], A_R + 65536 + 8192 + 4096 * b) for b in range(2)]
    RED = [at(f"RED{b}", [P, P], A_R + 65536 + 16384 + 512 * b) for b in range(2)]
    o = A_R
    QT2 = at("QT2", [P, 4, S], o); o += 16384
    KT2 = at("KT2", [P, S], o); o += 4096
    V2 = at("V2", [P, NT, P], o); o += 4096
    QI = at("QI", [P, 4, S], o); YC = at("YC", [P, 4, S], o); o += 16384
    KI = at("KI", [P, S], o); o += 4096
    SC = at("SC", [P, N_SCORE], o); o += 4 * N_SCORE
    MASK01 = at("MASK01", [P, 3 * P], o); o += 4 * 3 * P
    A_COS = o
    COS = at("COS", [P, S], o); o += 4096
    SIN = at("SIN", [P, S], o); o += 4096
    T2 = [at(f"T2_{b}", [P, S], o + 4096 * b) for b in range(2)]; o += 8192
    T1 = at("T1", [P, S], o); o += 4096
    assert o <= nc.sbuf_usable_end
    QS2 = [at(f"QS2_{h}", [P, S], at_h, F32R) for h, at_h in enumerate(
        [A_XH + 12288 + 4096 * n for n in range(3)] + [A_XL + 4096 * n for n in range(4)] + [A_R + 40960])]
    KS2 = [at(f"KS2_{r}", [P, S], A_COS + 4096 * r, F32R) for r in range(2)]
    KL2 = at("KL2", [P, S], A_COS + 8192, F32R)
    SQ2 = [at(f"SQ2_{b}", [P, S], A_R + 4096 * b) for b in range(2)]
    SSQ2 = at("SSQ2", [P, S], A_R + 8192)
    DG2 = at("DG2", [P, NT, P], A_R + 12288)
    HC = [at(f"HC{b}", [P, S], A_R + 45056 + 4096 * b) for b in range(2)]
    o = A_XT
    CU = at("CU", [P, 4, S + PAD], o); o += 16 * (S + PAD)
    SIG = at("SIG", [P, S], o); o += 4096
    JUNK = at("JUNK", [P, 2, S], o, U8); o += 2 * S
    TK1 = at("TK1", [P, S], o); POSI = at("POSI", [P, S], o, I32); o += 4096
    TK2 = at("TK2", [P, S], o); o += 4096
    assert o <= A_XH

    G = [nc.alloc_psum_tensor(f"G{b}", [P, 2, HALF], F32) for b in range(2)]
    TP = [nc.alloc_psum_tensor(f"TP{b}", [P, 2, HALF], F32) for b in range(2)]

    x_spill = nc.dram_tensor("x_spill", [D, S], F32, kind="Internal").ap()
    tab_spill = nc.dram_tensor("tab_spill", [HEADS * 2 * S], F32, kind="Internal").ap()
    tiled = lambda t: t.rearrange("(k p) t -> p k t", p=P)
    xT_v, spill_v, out_v = tiled(xT), tiled(x_spill), tiled(outT)

    RB = small("RB", 8)
    var = small("var", NT)
    root = small("root", NT)
    y0 = small("y0", NT)
    aa = small("aa", NT)
    rstd = small("rstd", NT)
    negm = small("negm", 3)
    den = small("den", 4)
    rden = small("rden", 2)
    bn6 = small("bn6", NT * 6)
    mv = small("mv", NT * 2)
    mod = small("mod", 48)
    scl = small("scl", 16)
    silc = small("silc", 8)
    wi = small("wi", NT * 8)
    NQ = NT - TOPK_TILE
    sgn = small("sgn", NQ)
    need = small("need", NQ)
    most = small("most", NQ)
    cnt = small("cnt", NQ)
    keep = small("keep", NQ, U32)
    mag = small("mag", NQ, U32)
    cand = small("cand", NQ, U32)
    thr = small("thr", NQ)
    above_mag = small("above_mag", NQ)

    raw_loaded = [sem(f"raw_loaded{b}") for b in range(2)]
    hi_ready, lo_ready = sem("hi_ready"), sem("lo_ready")
    slab_done = sem("slab_done")
    psum_free = [sem(f"psum_free{b}") for b in range(2)]
    params_loaded, x_loaded, sgu_loaded = sem("params_loaded"), sem("x_loaded"), sem("sgu_loaded")
    hot_loaded, tab_made, tab_stored = sem("hot_loaded"), sem("tab_made"), sem("tab_stored")
    tab_copied = sem("tab_copied")
    bias_loaded = [sem(f"bias_loaded{b}") for b in range(2)]
    x_hi, x_split = sem("x_hi"), sem("x_split")
    turned_in, turned, turn_out = sem("turned_in"), sem("turned"), sem("turn_out")
    sq_ready, sq_used = sem("sq_ready"), sem("sq_used")
    stat_ready, var_ready, root_ready = sem("stat_ready"), sem("var_ready"), sem("root_ready")
    diag_ready, spread_ready, hf_ready = sem("diag_ready"), sem("spread_ready"), sem("hf_ready")
    scores_ready, masked, exped = sem("scores_ready"), sem("masked"), sem("exped")
    half_turned, pt_a, pt_b = sem("half_turned"), sem("pt_a"), sem("pt_b")
    pv_done, att_out = sem("pv_done"), sem("att_out")
    stack_hi, stack_lo = sem("stack_hi"), sem("stack_lo")
    mixed_ready, mixed_mm, gated = sem("mixed_ready"), sem("mixed_mm"), sem("gated")
    dve_seq, act_seq, pool_seq = sem("dve_seq"), sem("act_seq"), sem("pool_seq")
    xre_loaded = [sem(f"xre_loaded{b}") for b in range(4)]
    xt_ready = sem("xt_ready")
    spilled, x_back = sem("spilled"), sem("x_back")
    usq_ready, u_hi, u_split = sem("usq_ready"), sem("u_hi"), sem("u_split")
    ada_loaded = [sem(f"ada_loaded{b}") for b in range(2)]
    ada_prod, ada_red, mod_col, mod_ready = sem("ada_prod"), sem("ada_red"), sem("mod_col"), sem("mod_ready")
    silc_ready = sem("silc_ready")
    pos_loaded, angle_ready, rope_ready = sem("pos_loaded"), sem("angle_ready"), sem("rope_ready")
    swapped, roped = sem("swapped"), sem("roped")
    raw_copied = sem("raw_copied")
    ki_doubled, wi_turned, wi_ready = sem("ki_doubled"), sem("wi_turned"), sem("wi_ready")
    idx_scores, idx_relu, idx_added, idx_masked = sem("idx_scores"), sem("idx_relu"), sem("idx_added"), sem("idx_masked")
    v2_turned, v2_ready = sem("v2_turned"), sem("v2_ready")
    cu_raw, sig_ready, glu_ready = sem("cu_raw"), sem("sig_ready"), sem("glu_ready")
    conv_ready, conv_mean, conv_centred = sem("conv_ready"), sem("conv_mean"), sem("conv_centred")
    cand_ready, act_counted = sem("cand_ready"), sem("act_counted")
    cleared, out_stored, mask01 = sem("cleared"), sem("out_stored"), sem("mask01")

    def V(name, k=0):
        c = VCOL[name] + k
        return vec[:, c:c + 1]

    flat = lambda t: t[:, :, :].rearrange("p a b -> p (a b)")
    Gf, TPf = [flat(t) for t in G], [flat(t) for t in TP]

    UNITS1 = [(i, h, NT) for h in range(HEADS) for i in range(NT)]
    UNITS2 = [(i, h, i + 1) for i in range(NT) for h in range(HEADS)]
    UNITS = UNITS1 + UNITS2
    n_b = [0]
    n_half = [0]
    for _, _, w in UNITS:
        n_b.append(n_b[-1] + (w > 4))
        n_half.append(n_half[-1] + 1 + (w > 4))

    ACT_TILES, DVE_TILES = (1, 2, 5), (0, 3, 4)
    bits_beside = {m: 2 if m <= 10 else 3 for m in range(5, 18)}
    bits_beside[17] = BITS - sum(v for m, v in bits_beside.items() if m < 17)

    def halves(h):
        a, b = slice(0, DH), slice(DH, P)
        return (b, a) if h % 2 else (a, b)

    STACKED_HI, STACKED_LO = 3 * HEADS, 2 * HEADS

    def taken(g):
        return psum_free[g % 2], g // 2 + 2

    def slabs_of(eng, g0, first, last, body):
        pairs = (last - first) // 2
        if pairs >= 2:
            with eng.Fori(0, pairs) as t:
                for j in range(2):
                    g = g0 + first + j
                    body(t * 2 + (first + j), t * 2 + g, g % 2, t + g // 2)
            first += 2 * pairs
        for m in range(first, last):
            g = g0 + m
            body(m, g, g % 2, g // 2)

    N_HF_BEFORE_OUT = 8 * 3 + 4

    block = ctx.enter_context(nc.Block())

    @block.sync
    def _(sp):
        def load(g, b):
            sp.dma_start(raw[b][:, :], slabs[bass.ds(g, 1), :, :].rearrange("a p n -> p (a n)")
                         if not isinstance(g, int) else slabs[g, :, :]).then_inc(raw_loaded[b], 16)

        load(0, 0)
        sp.dma_start(vec[:, :], vecs).then_inc(params_loaded, 16)
        sp.dma_start(cst[:, :], consts).then_inc(params_loaded, 16)
        for k in range(KT_N):
            sp.dma_start(XT[:, k, :], xT_v[:, k, :]).then_inc(x_loaded, 16)
        load(1, 1)
        with sp.Fori(0, (STREAM - 2) // 2) as t:
            for j in range(2):
                sp.wait_ge(lo_ready, t * 2 + (1 + j))
                load(t * 2 + (2 + j), j)
        sp.wait_ge(out_stored, 16 * KT_N)

    @block.gpsimd
    def _(pool):
        pseq = Tally(pool_seq)
        pool.dma_start(HOT[0:33, :], hot).then_inc(hot_loaded, 16)
        pool.wait_ge(cleared, 1)
        pool.dma_start(RB[0:32, :], rel_bias).then_inc(hot_loaded, 16)
        pool.wait_ge(tab_copied, 1)
        pool.dma_start(tab_spill.rearrange("(h n) -> h n", h=HEADS), TAB[0:HEADS, :]).then_inc(tab_stored, 16)
        pool.wait_ge(tab_stored, 16)
        pool.wait_ge(x_split, KT_N)

        def load_bias(h):
            src = bass.AP(tensor=tab_spill.tensor, offset=h * 2 * S + S - 896 - (P - 1),
                          ap=[[1, P], [1, 1920]])
            pool.dma_start(BIAS[h % 2][:, :], src).then_inc(bias_loaded[h % 2], 16)

        pool.dma_start(SGW[:, :, :], sgu_wT.rearrange("p (g t) -> p g t", g=SGU_G)).then_inc(sgu_loaded, 16)
        for r in range(2):
            pool.dma_start(LNG[:, r, :], lnrow[r:r + 1, :].broadcast_to([P, ATT])).then_inc(sgu_loaded, 16)
        for h in range(HEADS):
            if h >= 2:
                pool.wait_ge(masked, NT * (h - 1))
            load_bias(h)

        def residual_tiles(src):
            for k in range(KT_N):
                if k >= 4:
                    pool.wait_ge(xt_ready, base_xt[0] + k - 3)
                pool.dma_start(XRE[:, k % 4, :], src[:, k, :]).then_inc(xre_loaded[k % 4], 16)
            base_xt[0] += KT_N

        base_xt = [0]
        pool.wait_ge(x_split, 16)
        residual_tiles(xT_v)
        pool.wait_ge(xt_ready, KT_N)
        pool.dma_start(spill_v, XT[:, :, :]).then_inc(spilled, 16)

        def ada_load(a, b):
            pool.dma_start(ADA[b][:, :, :].rearrange("p k n -> p (k n)"),
                           ada[bass.ds(a, 1), :, :].rearrange("a p n -> p (a n)")
                           if not isinstance(a, int) else ada[a, :, :]).then_inc(ada_loaded[b], 16)

        pool.wait_ge(x_split, 24)
        pool.wait_ge(silc_ready, 1)
        ada_load(0, 0)
        ada_load(1, 1)
        with pool.Fori(0, 23) as t:
            for b in range(2):
                pool.wait_ge(ada_loaded[b], t * 16 + 16)
                pool.tensor_tensor(ADA[b][:, :, :], ADA[b][:, :, :],
                                   silc[:, :].unsqueeze(2).broadcast_to([P, KT_N, P]), ALU.mult).then_inc(ada_prod, 1)
                pool.wait_ge(ada_red, t * 2 + (1 + b))
                ada_load(t * 2 + (2 + b), b)
        for b in range(2):
            pool.wait_ge(ada_loaded[b], 16 * 24)
            pool.tensor_tensor(ADA[b][:, :, :], ADA[b][:, :, :],
                               silc[:, :].unsqueeze(2).broadcast_to([P, KT_N, P]), ALU.mult).then_inc(ada_prod, 1)
        pool.wait_ge(spilled, 16)
        pool.wait_ge(slab_done, 1 + IN2)
        residual_tiles(spill_v)
        pool.wait_ge(xt_ready, 2 * KT_N)
        pool.dma_start(spill_v, XT[:, :, :]).then_inc(spilled, 16)
        pool.wait_ge(x_split, 32)
        pool.wait_ge(spilled, 32)
        pool.dma_start(POSI[:, :], positions.broadcast_to([P, S])).then_inc(pos_loaded, 16)
        pool.memset(CU[:, :, 0:PAD], 0.0).then_inc(pool_seq, 1); pseq.n += 1
        pool.memset(MASK01[:, :], 0.0).then_inc(pool_seq, 1); pseq.n += 1
        pseq.wait(pool)
        for c in (0, 2):
            pool.affine_select(out=MASK01[:, c * P:(c + 1) * P], in_=MASK01[:, c * P:(c + 1) * P], compare_op=ALU.is_ge,
                               fill=-FAR, base=0, pattern=[[-1, P]], channel_multiplier=1).then_inc(mask01, 1)
        pool.wait_ge(roped, 1)
        pool.dma_start(KI[DH:P, :], KI[0:DH, :]).then_inc(ki_doubled, 16)
        for n, i in enumerate(range(TOPK_TILE, NT)):
            pool.wait_ge(idx_added, HEADS * (n + 1))
            c = score_at(i) + P * i
            pool.affine_select(out=SC[:, c:c + P], in_=SC[:, c:c + P], compare_op=ALU.is_ge,
                               fill=LOWEST, base=0, pattern=[[-1, P]], channel_multiplier=1).then_inc(idx_masked, 1)
        pool.wait_ge(conv_ready, 4)
        pool.dma_start(XT[:, :, :], spill_v).then_inc(x_back, 16)
        for k in range(KT_N):
            pool.wait_ge(hf_ready, N_HF_BEFORE_OUT + k + 1)
            pool.dma_start(out_v[:, k, :], XT[:, k, :]).then_inc(out_stored, 16)
        pool.wait_ge(out_stored, 16 * KT_N)

    @block.scalar
    def _(act):
        aseq = Tally(act_seq)
        t_sqi, t_squ = Tally(sq_ready), Tally(sq_used)
        t_var, t_root = Tally(var_ready), Tally(root_ready)
        t_hf = Tally(hf_ready)

        def hi(g, b, h):
            act.wait_ge(raw_loaded[b], h * 16 + 16)
            if not (isinstance(g, int) and g < 2):
                act.wait_ge(slab_done, g)
            act.activation(whi[b][:, :, :].rearrange("p k n -> p (k n)"), raw[b][:, :], ACT.Copy).then_inc(hi_ready, 1)

        def hi_next(g, b, h):
            hi(g + 1, 1 - b, h + (1 if b else 0))

        def square(k, src, wait, sq=SQ):
            act.wait_ge(*wait)
            if t_sqi.n >= 2:
                act.wait_ge(sq_used, t_sqi.n - 1)
            t_sqi.inc(act.activation(sq[k % 2][:, :], src[:, k, :], ACT.Square))

        def squares(src, wait):
            for k in range(KT_N):
                square(k, src, wait(k))

        def norm_root():
            t_var.wait(act, 1)
            t_root.inc(act.activation(root[:, :], var[:, :], ACT.Sqrt))

        def splits(n, dst, bias=None, func=ACT.Identity, scale=None):
            for k in range(n):
                t_hf.wait(act, 1)
                act.activation(XH[:, dst + k, :], HF[k % 2][:, :], ACT.Identity,
                               bias=bias(k) if bias else 0.0).then_inc(x_hi, 1)

        act.wait_ge(params_loaded, 32)
        hi(0, 0, 0)
        squares(XT, lambda k: (x_loaded, 16 * KT_N))
        norm_root()
        act.wait_ge(params_loaded, 32)
        act.activation(silc[:, :], vec[:, VCOL["c"]:VCOL["c"] + 8], ACT.Silu).then_inc(silc_ready, 1)
        splits(KT_N, 0)

        def to_qk(dst, scale, off):
            def body(m, g, b, h):
                hi_next(g, b, h)
                act.wait_ge(slab_done, g + 2)
                act.activation(dst[:, bass.ds(m + (-off), 1), :].rearrange("p a t -> p (a t)")
                               if not isinstance(m, int) else dst[:, m - off, :],
                               Gf[b], ACT.Copy, scale=scale).then_inc(psum_free[b], 1)
            return body

        def to_tt(func, n0):
            def body(m, g, b, h):
                hi_next(g, b, h)
                act.wait_ge(slab_done, g + 2)
                if not (isinstance(m, int) and m - n0 < 2):
                    act.wait_ge(turned, m + (-n0 - 1))
                act.activation(TT[b][:, :], Gf[b], func).then_inc(psum_free[b], 1)
            return body

        slabs_of(act, IN1, 0, 2, to_tt(ACT.Gelu_apprx_tanh, 0))
        slabs_of(act, IN1, 2, 8, to_tt(ACT.Gelu_apprx_tanh, 0))
        for m in range(4):
            g = IN1 + S_Q1 + m
            hi_next(g, g % 2, g // 2)
            act.wait_ge(slab_done, g + 2)
            act.activation(QT[:, m, :].rearrange("p (t c) -> p t c", c=P)[:, :, ::-1],
                           Gf[g % 2].rearrange("p (t c) -> p t c", c=P), ACT.Copy,
                           scale=-DH ** -0.5).then_inc(psum_free[g % 2], 1)
            if m == 2:
                norm_root()
        slabs_of(act, IN1, S_K1, S_V1, to_qk(KT, 1.0, S_K1))

        def stack(h):
            own, other = halves(h)
            if h >= 2:
                act.wait_ge(scores_ready, NT * (h - 1))
            for dst, src, at_p in ((QS, QT, own), (KS, KT, own), (KS, KT, other)):
                act.activation(dst[h % 2][at_p, :], src[own, h // 2, :], ACT.Copy).then_inc(stack_hi, 1)

        slabs_of(act, IN1, S_V1, S_V1 + 1, to_tt(ACT.Copy, 8))
        slabs_of(act, IN1, S_V1 + 1, S_V1 + 2, to_tt(ACT.Copy, 8))
        act.wait_ge(gated, SGU_G)
        act.wait_ge(psum_free[1], (IN1 + S_V1 + 1) // 2 + 2)
        stack(0)
        slabs_of(act, IN1, S_V1 + 2, S_V1 + 4, to_tt(ACT.Copy, 8))

        def attention(n0, n1):
            def exp(n):
                w = UNITS[n][2] * P
                act.wait_ge(masked, n + 1)
                act.activation(PB[n % 3][:, 0:w], PB[n % 3][:, 0:w], ACT.Exp, bias=negm[:, n % 3:n % 3 + 1], scale=-1.0,
                               accum_out=den[:, n % 4:n % 4 + 1]).then_inc(exped, 1)

            def copy_a(n):
                w = min(UNITS[n][2], 4) * P
                act.wait_ge(half_turned, n_half[n] + 1)
                if n >= 2:
                    act.wait_ge(pv_done, n - 1)
                act.activation(PTS[n % 2][:, 0:w], TPf[0][:, 0:w], ACT.Copy).then_inc(pt_a, 1)

            def copy_b(n):
                w = UNITS[n][2] * P
                if w > 4 * P:
                    act.wait_ge(half_turned, n_half[n + 1])
                    act.activation(PTS[n % 2][:, 4 * P:w], TPf[0][:, 4 * P:w], ACT.Copy).then_inc(pt_b, 1)

            for n in range(n0, n1 + 2):
                if n >= n0 + 2:
                    copy_a(n - 2)
                    if n0:
                        copy_b(n - 2)
                if n < n1:
                    exp(n)
                if n < 56 and n % NT == 2:
                    stack(n // NT + 1)

        act.wait_ge(slab_done, 1 + OUT1)
        attention(0, 64)

        def turned_hi(k0, n, base):
            for k in range(n):
                act.wait_ge(turned, base + k + 1)
                act.activation(XH[:, k0 + k, :], TPf[(base + k) % 2], ACT.Copy).then_inc(x_hi, 1)

        turned_hi(0, 8, 12)

        def out_squares(g0, src):
            for m in range(8):
                g = g0 + m
                hi_next(g, g % 2, g // 2)
                if m:
                    square(m - 1, src, taken(g - 1))
            square(7, src, taken(g))

        out_squares(OUT1, ACC)
        norm_root()
        hi_next(FFN1, FFN1 % 2, FFN1 // 2)
        for k in range(KT_N):
            act.wait_ge(xt_ready, k + 1)
            act.activation(XH[:, k, :], XT[:, k, :], ACT.Identity, scale=V("g_pre_ffn", k), bias=0.0).then_inc(x_hi, 1)
        squares(XT, lambda k: (xt_ready, 1 + k))
        norm_root()

        def ffn(g0, which):
            def group(grp, last=False):
                for m in range(16):
                    g, b = g0 + m, (g0 + m) % 2
                    h = grp * 8 + g // 2
                    if not (which == 0 and isinstance(grp, int) and grp == 0 and m == 0):
                        hi(grp * 16 + (g + 1), 1 - b, h + (1 if b else 0))
                    if m < 8:
                        u = grp * 8 + (32 * which + m)
                        if which == 0:
                            act.wait_ge(psum_free[b], grp * 8 + (g // 2 + 2))
                            act.activation(RELU[:, :], RELU[:, :], ACT.Square).then_inc(usq_ready, 1)
                        else:
                            act.wait_ge(slab_done, grp * 16 + (g + 2))
                            act.wait_ge(usq_ready, u + 1)
                            act.activation(RELU[:, :], Gf[b], ACT.Relu).then_inc(psum_free[b], 1)
                        act.wait_ge(usq_ready, u + 2)
                        act.activation(UH[:, m, :], (USQ if which else RELU)[:, :], ACT.Copy).then_inc(u_hi, 1)
                    elif last and m > 8:
                        square(m - 9, XT, taken(grp * 16 + g - 1), SQF)

            if which == 0:
                group(0)
            with act.Fori(1 - which, GROUPS - 1) as grp:
                group(grp)
            group(GROUPS - 1, last=True)
            square(7, XT, taken(g0 + 16 * GROUPS - 1), SQF)

        ffn(FFN1, 0)
        norm_root()
        act.wait_ge(slab_done, 1 + IN2)
        squares(XT, lambda k: (xt_ready, 1 + KT_N + k))
        norm_root()
        act.wait_ge(mod_ready, 1)
        splits(KT_N, 0, lambda k: mod[:, k:k + 1])

        hi_next(IN2, IN2 % 2, IN2 // 2)
        for tab in (COS, SIN):
            act.wait_ge(angle_ready, 1 if tab is COS else 2)
            act.activation(tab[:, :], tab[:, :], ACT.Sin).then_inc(rope_ready, 1)

        def step(m, func=ACT.Copy, scale=1.0, dst=None, waits=()):
            g = IN2 + m
            if m:
                hi_next(g, g % 2, g // 2)
            act.wait_ge(slab_done, g + 2)
            for s, v in waits:
                act.wait_ge(s, v)
            act.activation(dst, Gf[g % 2], func, scale=scale).then_inc(psum_free[g % 2], 1)

        N_ROPED = 10
        for m in range(5):
            step(m, dst=T2[m % 2][:, :], waits=([(roped, m - 1)] if m >= 2 else []) + ([(wi_turned, 1)] if m == 2 else []))
        n = 0
        for i in range(TOPK_TILE, NT):
            for h in range(HEADS):
                act.wait_ge(idx_scores, n + 1)
                if n >= 2:
                    act.wait_ge(idx_added, n - 1)
                act.activation(T2[n % 2][:, 0:P * (i + 1)], Gf[n % 2][:, 0:P * (i + 1)], ACT.Relu,
                               scale=DH ** -0.5).then_inc(idx_relu, 1)
                n += 1
        act.wait_ge(idx_added, HEADS * NQ)
        t_bit, t_counted = Tally(cand_ready), Tally(act_counted)

        def count_signs(bits):
            for _ in range(bits):
                t_bit.wait(act, 1)
                for n in ACT_TILES:
                    w = P * (TOPK_TILE + n + 1)
                    if t_counted.n >= 2:
                        act.wait_ge(act_counted, t_counted.n - 1)
                    t_counted.inc(act.activation((TK1, TK2)[t_counted.n % 2][:, 0:w],
                                                 SC[:, score_at(TOPK_TILE + n):score_at(TOPK_TILE + n + 1)], ACT.Sign,
                                                 scale=-1.0, bias=cand[:, n:n + 1].bitcast(F32),
                                                 accum_out=cnt[:, n:n + 1]))

        for m in range(5, N_IN2):
            if m < S_CONV:
                step(m, dst=T2[m % 2][:, :], scale=-DH ** -0.5 if m < S_K else 1.0, waits=[(roped, m - 1)])
            else:
                j, gate = divmod(m - S_CONV, 2)
                if gate:
                    step(m, dst=SIG[:, :], func=ACT.Sigmoid, waits=[(glu_ready, j)] if j else [])
                else:
                    step(m, dst=CU[:, j, PAD:PAD + S])
            count_signs(bits_beside.get(m, 0))
        act.wait_ge(slab_done, 1 + OUT2)
        act.wait_ge(roped, 10)
        act.wait_ge(v2_ready, 1)
        for r in range(2):
            for at_p in halves(r):
                act.activation(KS2[r][at_p, :], KT2[halves(r)[0], :], ACT.Copy).then_inc(stack_hi, 1)
        for h in range(HEADS):
            own = halves(h // 4)[0]
            act.activation(QS2[h][own, :], QT2[own, h % 4, :], ACT.Copy).then_inc(stack_hi, 1)
        attention(64, 128)
        turned_hi(0, 4, 20)
        for j in range(4):
            act.wait_ge(conv_centred, j + 1)
            act.wait_ge(sq_used, t_sqi.n - 1)
            t_sqi.inc(act.activation(SQ2[j % 2][:, :], YC[:, j, :], ACT.Square))
        norm_root()
        for j in range(4):
            t_hf.wait(act, 1)
            if j >= 2:
                act.wait_ge(x_split, 36 + j - 1)
            act.activation(HC[j % 2][:, :], YC[:, j, :], ACT.Silu, scale=V("conv_g", j),
                           bias=V("conv_nb", j)).then_inc(act_seq, 1)
            aseq.n += 1
            aseq.wait(act)
            act.activation(XH[:, 4 + j, :], HC[j % 2][:, :], ACT.Copy).then_inc(x_hi, 1)

        out_squares(OUT2, XT)
        norm_root()
        splits(KT_N, 0, lambda k: mod[:, 24 + k:25 + k])
        ffn(FFN2, 1)
        norm_root()

    @block.tensor
    def _(pe):
        t_sq, t_stat = Tally(sq_used), Tally(stat_ready)
        t_diag, t_spread = Tally(diag_ready), Tally(spread_ready)

        def product(g, b, h, xh, xl, fresh=None, base=0, before_last=None):
            pe.wait_ge(lo_ready, g + 1)
            pe.wait_ge(psum_free[b], h + 1)
            for k in range(KT_N):
                if fresh is not None:
                    pe.wait_ge(fresh, base + k + 1)
                if before_last and k == KT_N - 1:
                    before_last()
                for n, (w, x) in enumerate(((whi, xh), (whi, xl), (wlo, xh))):
                    for half in range(2):
                        last = pe.matmul(G[b][:, half, :], w[b][:, k, :], x[:, k, half * HALF:(half + 1) * HALF],
                                         start=(k == 0 and n == 0), stop=(k == KT_N - 1 and n == 2))
            last.then_inc(slab_done, 1)

        def norm_stat(tiles, ssq):
            t_sq.wait(pe, tiles)
            for t in range(NT):
                last = pe.matmul(TP[1][:, 0, t:t + 1], ssq[:, t * P:(t + 1) * P], ones[:, 0:1], start=True, stop=True)
            t_stat.inc(last)

        def norm_spread(dg):
            t_diag.wait(pe, 1)
            for half in range(2):
                last = pe.matmul(TP[0][:, half, :], ones, dg[:, half * 4:half * 4 + 4, :].rearrange("p t n -> p (t n)"),
                                 start=True, stop=True)
            t_spread.inc(last)

        def norm(tiles=KT_N, ssq=SSQ, dg=DG):
            norm_stat(tiles, ssq)
            norm_spread(dg)

        pe.wait_ge(params_loaded, 32)
        pe.wait_ge(hot_loaded, 32)
        for c in range(4):
            last = pe.matmul(G[c // 2][0:HEADS, c % 2, :], RB[0:33, :], HOT[0:33, c * HALF:(c + 1) * HALF],
                             start=True, stop=True)
        last.then_inc(tab_made, 1)
        norm()
        pe.wait_ge(tab_copied, 1)

        x1 = lambda m, g, b, h: product(g, b, h, XH, XL)
        product(IN1, 0, 0, XH, XL, x_split, 0)

        def turn(b, h, n, par):
            pe.wait_ge(psum_free[b], h + 2)
            if not (isinstance(n, int) and n < 2):
                pe.wait_ge(turn_out, n + (-1))
            for t in range(NT):
                last = pe.transpose(TP[par][:, t // 4, (t % 4) * P:(t % 4 + 1) * P], TT[b][:, t * P:(t + 1) * P], ident)
            last.then_inc(turned, 1)

        def with_turn(n0):
            def body(m, g, b, h):
                product(g, b, h, XH, XL)
                turn(1 - b, h + (0 if b else -1), m + (-1 - n0), 1 - b)
            return body

        slabs_of(pe, IN1, 1, 3, with_turn(0))
        slabs_of(pe, IN1, 3, 9, with_turn(0))
        slabs_of(pe, IN1, 9, 13, x1)
        for m in range(13, 17):
            product(IN1 + m, m % 2, m // 2, XH, XL)
            if m == 13:
                pe.wait_ge(turn_out, 8)
                pe.wait_ge(sgu_loaded, 48)
                pe.wait_ge(mixed_ready, 1)
            for g in (2 * m - 26, 2 * m - 25):
                if g >= 2:
                    pe.wait_ge(gated, g - 1)
                pe.matmul(TP[g % 2][:, 0, :], SGW[:, g, :], NAT[:, 1, :, g * DH:(g + 1) * DH],
                          start=True, stop=True).then_inc(mixed_mm, 1)
        product(IN1 + 17, 1, 8, XH, XL)
        pe.wait_ge(gated, SGU_G)
        turn(0, 8, 8, 0)
        for m in range(18, 20):
            with_turn(8)(m, IN1 + m, m % 2, m // 2)
        turn(1, 9, 11, 1)
        pe.wait_ge(turn_out, 12)

        def attention(n0, n1, ops):
            def scores(n):
                i, h, w = UNITS[n]
                pairs, _ = ops(i, h)
                if n >= n0 + 2:
                    pe.wait_ge(masked, n - 1)
                for c in range(0, w, 4):
                    cw = min(4, w - c) * P
                    for r, (q, k) in enumerate(pairs):
                        last = pe.matmul(G[n % 2][:, c // 4, 0:cw], q, k[:, c * P:c * P + cw],
                                         start=(r == 0), stop=(r == len(pairs) - 1))
                last.then_inc(scores_ready, 1)

            def turns(n):
                w = UNITS[n][2]
                pe.wait_ge(exped, n + 1)
                for half in range(2 if w > 4 else 1):
                    if half and n_b[n]:
                        pe.wait_ge(pt_b, n_b[n])
                    elif n:
                        pe.wait_ge(pt_a, n)
                    for c in range(4 * half, min(w, 4 * half + 4)):
                        last = pe.transpose(TP[0][:, half, (c % 4) * P:(c % 4 + 1) * P],
                                            PB[n % 3][:, c * P:(c + 1) * P], ident)
                    last.then_inc(half_turned, 1)

            def values(n):
                i, h, w = UNITS[n]
                v = ops(i, h)[1]
                pe.wait_ge(pt_a, n + 1)
                if w > 4:
                    pe.wait_ge(pt_b, n_b[n + 1])
                if n >= 2:
                    pe.wait_ge(att_out, n - 1)
                for c in range(w):
                    last = pe.matmul(TP[1][:, n % 2, 0:DH], PTS[n % 2][:, c * P:(c + 1) * P], v(c),
                                     start=(c == 0), stop=(c == w - 1))
                last.then_inc(pv_done, 1)

            for n in range(n0, n1 + 3):
                if n < n1:
                    scores(n)
                if n0 + 2 <= n < n1 + 2:
                    turns(n - 2)
                if n >= n0 + 3:
                    values(n - 3)

        def ops1(i, h):
            own, tile = halves(h)[0], slice(i * P, (i + 1) * P)
            if i == 0:
                pe.wait_ge(stack_hi, 3 * (h + 1))
                pe.wait_ge(stack_lo, 2 * (h + 1))
            return (((QS[h % 2][:, tile], KS[h % 2]), (QS[h % 2][own, tile], KL[own, :])),
                    lambda c: NAT[:, 2, c, h * DH:(h + 1) * DH])

        attention(0, 64, ops1)

        def turn_mixed(src, n, base, xbase, flipped=0):
            for k in range(n):
                if k >= 2:
                    pe.wait_ge(x_split, xbase + k - 1)
                for t in range(NT):
                    dst = TP[(base + k) % 2][:, t // 4, (t % 4) * P:(t % 4 + 1) * P]
                    if k < flipped:
                        last = pe.matmul(dst, src(k, t), flip, start=True, stop=True)
                    else:
                        last = pe.transpose(dst, src(k, t), ident)
                last.then_inc(turned, 1)

        pe.wait_ge(att_out, 64)
        turn_mixed(lambda k, t: NATA[:, t, k * P:(k + 1) * P] if k < 4 else NAT[:, 0, t, (k - 4) * P:(k - 3) * P],
                   8, 12, 8, flipped=4)
        product(OUT1, OUT1 % 2, OUT1 // 2, XH, XL, x_split, 8)
        slabs_of(pe, OUT1, 1, 8, x1)
        norm()

        def ffn(g0, which, xbase):
            def ada_sum(grp, a):
                pe.wait_ge(ada_red, grp * 12 + (a + 1))
                col = grp * 12 + a
                pe.matmul(TP[1][:, 1, col:col + 1] if isinstance(col, int) else TP[1][:, 1, bass.ds(col, 1)], RED[a % 2][:, :], ones[:, 0:1],
                          start=True, stop=True).then_inc(mod_col, 1)

            def group(grp, m0=0):
                for m in range(m0, 16):
                    g, b = g0 + m, (g0 + m) % 2
                    up = m < 8
                    product(grp * 16 + g, b, grp * 8 + g // 2, XH if up else UH, XL if up else UL,
                            *((x_split, xbase) if m == 0 else (u_split, grp * 8 + 32 * which) if m == 8 else ()))
                    if which == 0 and (up or m % 2):
                        a = m if up else 8 + (m - 8) // 2
                        for late in range(m0 if m == m0 else 0):
                            ada_sum(grp, late)
                        ada_sum(grp, a)

            if which == 0:
                product(g0, g0 % 2, g0 // 2, XH, XL, x_split, xbase)
                product(g0 + 1, (g0 + 1) % 2, (g0 + 1) // 2, XH, XL, before_last=lambda: norm_stat(KT_N, SSQ))
                norm_spread(DG)
                group(0, 2)
            with pe.Fori(1 - which, GROUPS - 1) as grp:
                group(grp)
            group(GROUPS - 1)

        ffn(FFN1, 0, 16)
        norm(KT_N, SSQF, DGF)
        norm()

        def swap_pairs(m):
            g = IN2 + m
            pe.wait_ge(psum_free[g % 2], g // 2 + 2)
            if m:
                pe.wait_ge(roped, m)
            for half in range(2):
                last = pe.matmul(TP[0][:, half, :], swap, T2[m % 2][:, half * HALF:(half + 1) * HALF],
                                 start=True, stop=True)
            last.then_inc(swapped, 1)

        for m in range(5):
            g = IN2 + m
            product(g, g % 2, g // 2, XH, XL, *((x_split, 24) if m == 0 else ()))
            if m:
                swap_pairs(m - 1)
            if m == 1:
                for t in range(NT):
                    last = pe.transpose(TP[1][:, 0, t * 8:t * 8 + 8], T2[0][DH:DH + 8, t * P:(t + 1) * P],
                                        ident[DH:DH + 8, DH:DH + 8])
                last.then_inc(wi_turned, 1)
        swap_pairs(4)
        pe.wait_ge(roped, 5)
        pe.wait_ge(ki_doubled, 16)
        n = 0
        for i in range(TOPK_TILE, NT):
            for h in range(HEADS):
                at_p = slice((h % 2) * DH, (h % 2 + 1) * DH)
                if n >= 2:
                    pe.wait_ge(idx_relu, n - 1)
                for c in range(0, i + 1, 4):
                    cw = min(4, i + 1 - c) * P
                    last = pe.matmul(G[n % 2][:, c // 4, 0:cw], QI[at_p, h // 2, i * P:(i + 1) * P],
                                     KI[at_p, c * P:c * P + cw], start=True, stop=True)
                last.then_inc(idx_scores, 1)
                n += 1
        pe.wait_ge(idx_relu, n)
        for m in range(5, 19):
            g = IN2 + m
            product(g, g % 2, g // 2, XH, XL)
            if 6 <= m <= 10:
                swap_pairs(m - 1)
            if m == 11:
                pe.wait_ge(psum_free[(g - 1) % 2], (g - 1) // 2 + 2)
                for t in range(NT):
                    last = pe.transpose(TP[1][:, t // 4, (t % 4) * P:(t % 4 + 1) * P], T2[0][:, t * P:(t + 1) * P], ident)
                last.then_inc(v2_turned, 1)

        def ops2(i, h):
            own, tile = halves(h // 4)[0], slice(i * P, (i + 1) * P)
            if i == 0:
                pe.wait_ge(stack_hi, STACKED_HI + 4 + h + 1)
                pe.wait_ge(stack_lo, STACKED_LO + 2 + h + 1)
            return (((QS2[h][:, tile], KS2[h // 4]), (QS2[h][own, tile], KL2[own, :])),
                    lambda c: V2[:, c, (h // 4) * DH:(h // 4 + 1) * DH])

        pe.wait_ge(roped, 10)
        pe.wait_ge(v2_ready, 1)
        pe.wait_ge(glu_ready, 4)
        attention(64, 128, ops2)
        pe.wait_ge(att_out, 128)
        turn_mixed(lambda k, t: NATA[:, t, k * P:(k + 1) * P], 4, 20, 32)
        pe.wait_ge(x_split, 36)
        pe.wait_ge(conv_ready, 4)
        for half in range(2):
            for j in range(4):
                last = pe.matmul(TP[1][:, half, :], ones, YC[:, j, half * HALF:(half + 1) * HALF],
                                 start=(j == 0), stop=(j == 3))
        last.then_inc(conv_mean, 1)
        norm(4, SSQ2, DG2)
        product(OUT2, OUT2 % 2, OUT2 // 2, XH, XL, x_split, 32)
        slabs_of(pe, OUT2, 1, 8, x1)
        norm()
        ffn(FFN2, 1, 40)
        norm(KT_N, SSQF, DGF)

    @block.vector
    def _(dve):
        d = Tally(dve_seq)
        t_sq, t_squ = Tally(sq_ready), Tally(sq_used)
        t_stat, t_var, t_root = Tally(stat_ready), Tally(var_ready), Tally(root_ready)
        t_diag, t_spread, t_hf = Tally(diag_ready), Tally(spread_ready), Tally(hf_ready)
        t_xt = Tally(xt_ready)

        def seq(ins):
            d.inc(ins)
            d.wait(dve)

        dve.memset(RB[0:33, :], 1.0).then_inc(cleared, 1)
        for n, s in enumerate((slab_done, psum_free[0], psum_free[1], usq_ready, mod_col, mod_col)):
            dve.memset(keep[:, n:n + 1], 0).then_inc(s, 1)

        def lo(g, b):
            dve.wait_ge(hi_ready, g + 1)
            dve.tensor_tensor(wlo[b][:, :, :].rearrange("p k n -> p (k n)"), raw[b][:, :],
                              whi[b][:, :, :].bitcast(F32).rearrange("p k n -> p (k n)"), ALU.subtract).then_inc(lo_ready, 1)

        def add_square(k, sq=SQ, ssq=SSQ):
            t_sq.wait(dve, 1)
            if k == 0:
                t_squ.inc(dve.tensor_copy(ssq[:, :], sq[0][:, :]))
            else:
                t_squ.wait(dve)
                t_squ.inc(dve.tensor_tensor(ssq[:, :], ssq[:, :], sq[k % 2][:, :], ALU.add))

        def reciprocal_root():
            t_root.wait(dve, 1)
            seq(dve.reciprocal(y0[:, :], root[:, :]))
            seq(dve.tensor_tensor(aa[:, :], y0[:, :], y0[:, :], ALU.mult))
            seq(dve.tensor_tensor(aa[:, :], aa[:, :], var[:, :], ALU.mult))
            seq(dve.tensor_scalar(aa[:, :], aa[:, :], -0.5, 1.5, ALU.mult, ALU.add))
            seq(dve.tensor_tensor(rstd[:, :], y0[:, :], aa[:, :], ALU.mult))

        def norm(width, eps, tiles=KT_N, sq=SQ, ssq=SSQ, dg=DG, first=0):
            for k in range(first, tiles):
                add_square(k, sq, ssq)
            t_stat.wait(dve, 1)
            t_var.inc(dve.tensor_scalar(var[:, :], TP[1][:, 0, 0:NT], 1.0 / width, eps, ALU.mult, ALU.add))
            t_var.wait(dve)
            reciprocal_root()
            t_diag.inc(dve.tensor_tensor(dg[:, :, :], ident.unsqueeze(1).broadcast_to([P, NT, P]),
                                         rstd[:, :].unsqueeze(2).broadcast_to([P, NT, P]), ALU.mult))
            t_spread.wait(dve, 1)

        def split_norm(scale, bias, base):
            def low(k):
                dve.wait_ge(x_hi, base + k + 1)
                hi_part = XH[:, k, :].bitcast(F32)
                if bias is None:
                    dve.tensor_tensor(XL[:, k, :], HF[k % 2][:, :], hi_part, ALU.subtract).then_inc(x_split, 1)
                else:
                    dve.scalar_tensor_tensor(out=XL[:, k, :], in0=HF[k % 2][:, :], scalar=bias(k), in1=hi_part,
                                             op0=ALU.add, op1=ALU.subtract).then_inc(x_split, 1)

            for k in range(KT_N):
                if k >= 2:
                    dve.wait_ge(x_split, base + k - 1)
                t_hf.inc(dve.scalar_tensor_tensor(out=HF[k % 2][:, :], in0=XT[:, k, :], scalar=scale(k), in1=TPf[0],
                                                  op0=ALU.mult, op1=ALU.mult))
                if k:
                    low(k - 1)
            t_hf.wait(dve)
            low(KT_N - 1)

        def residual(src, gain, n0, behind=None):
            for k in range(KT_N):
                seq(dve.scalar_tensor_tensor(out=src[:, k, :], in0=src[:, k, :], scalar=gain(k), in1=TPf[0],
                                             op0=ALU.mult, op1=ALU.mult))
                dve.wait_ge(xre_loaded[k % 4], 16 * (n0 + k // 4 + 1))
                t_xt.inc(dve.tensor_tensor(XT[:, k, :], src[:, k, :], XRE[:, k % 4, :], ALU.add))
                if behind and k:
                    behind(k - 1)
            if behind:
                behind(KT_N - 1)

        dve.wait_ge(tab_made, 1)
        for b in range(2):
            last = dve.tensor_scalar(TAB[0:HEADS, b * S:(b + 1) * S], Gf[b][0:HEADS, :], -1.0, None, ALU.mult)
        last.then_inc(tab_copied, 1)
        lo(0, 0)
        norm(D, RMS_EPS)
        dve.wait_ge(tab_stored, 16)
        split_norm(lambda k: V("g_pre_mix", k), None, 0)

        def only_lo(m, g, b, h):
            lo(g + 1, 1 - b)

        def turned_tile(n):
            dve.wait_ge(turned, n + 1)
            dve.tensor_copy(NAT[:, n // 4, :, (n % 4) * P:(n % 4 + 1) * P],
                            TPf[n % 2].rearrange("p (t c) -> p t c", t=NT)).then_inc(turn_out, 1)

        mv3 = mv[:, :].rearrange("p (t c) -> p t c", c=2)

        def sgu_norm():
            dve.wait_ge(turn_out, 8)
            for t in range(NT):
                seq(dve.bn_stats(bn6[:, 6 * t:6 * t + 6], NAT[:, 1, t, :]))
                last = dve.bn_aggr(mv[:, 2 * t:2 * t + 2], bn6[:, 6 * t:6 * t + 6])
            seq(last)
            t_var.inc(dve.tensor_scalar(var[:, :], mv3[:, :, 1], SGU_EPS, None, ALU.add))
            t_var.wait(dve)
            reciprocal_root()
            for t in range(NT):
                last = dve.tensor_scalar(NAT[:, 1, t, :], NAT[:, 1, t, :], mv3[:, t, 0:1], rstd[:, t:t + 1],
                                         ALU.subtract, ALU.mult)
            seq(last)

        def sgu_affine(r, op):
            last = dve.tensor_tensor(NAT[:, 1, :, :], NAT[:, 1, :, :],
                                     LNG[:, r, :].unsqueeze(1).broadcast_to([P, NT, ATT]), op)
            if r == 0:
                seq(last)
            else:
                last.then_inc(mixed_ready, 1)

        def gate(g):
            dve.wait_ge(mixed_mm, g + 1)
            z = NAT[:, 0, :, g * DH:(g + 1) * DH]
            dve.scalar_tensor_tensor(out=z, in0=TP[g % 2][:, 0, :].rearrange("p (n c) -> p n c", n=NT),
                                     scalar=V("sgu_b", g), in1=z, op0=ALU.add, op1=ALU.mult).then_inc(gated, 1)

        def stack_low(h):
            own, other = halves(h)
            dve.wait_ge(stack_hi, 3 * h + 2)
            if h >= 2:
                dve.wait_ge(scores_ready, NT * (h - 1))
            dve.tensor_tensor(QS[h % 2][other, :], QT[own, h // 2, :], QS[h % 2][own, :].bitcast(F32),
                              ALU.subtract).then_inc(stack_lo, 1)
            dve.tensor_tensor(KL[own, :], KT[own, h // 2, :], KS[h % 2][own, :].bitcast(F32),
                              ALU.subtract).then_inc(stack_lo, 1)

        for m in range(20):
            lo(IN1 + m + 1, (m + 1) % 2)
            if 2 <= m < 10:
                turned_tile(m - 2)
            if m == 10:
                sgu_norm()
                dve.wait_ge(sgu_loaded, 48)
            if m == 11:
                sgu_affine(0, ALU.mult)
            if m == 12:
                sgu_affine(1, ALU.add)
            if 13 <= m < 17:
                gate(2 * m - 26)
                gate(2 * m - 25)
            if m == 18:
                stack_low(0)
            if m >= 18:
                turned_tile(m - 10)
        turned_tile(10)
        turned_tile(11)

        def attention(n0, n1, bias_of, meanwhile=None):
            def mask(n):
                i, h, w = UNITS[n]
                bias = bias_of(n)
                dve.wait_ge(scores_ready, n + 1)
                if n >= 3:
                    dve.wait_ge(half_turned, n_half[n - 2])
                dve.tensor_tensor_reduce(out=PB[n % 3][:, 0:w * P], in0=Gf[n % 2][:, 0:w * P], in1=bias, scale=1.0,
                                         scalar=HIGHEST, op0=ALU.add, op1=ALU.min,
                                         accum_out=negm[:, n % 3:n % 3 + 1]).then_inc(masked, 1)

            def copy_b(n):
                w = (UNITS[n][2] - 4) * P
                if w > 0:
                    dve.wait_ge(half_turned, n_half[n + 1])
                    if n >= 2:
                        dve.wait_ge(pv_done, n - 1)
                    dve.tensor_copy(PTS[n % 2][:, 4 * P:4 * P + w], TPf[0][:, 4 * P:4 * P + w]).then_inc(pt_b, 1)

            def out(n):
                i, h, _ = UNITS[n]
                dve.wait_ge(pv_done, n + 1)
                seq(dve.reciprocal(rden[:, n % 2:n % 2 + 1], den[:, n % 4:n % 4 + 1]))
                dve.tensor_scalar(NATA[:, i, h * DH:(h + 1) * DH], TP[1][:, n % 2, 0:DH], rden[:, n % 2:n % 2 + 1], None,
                                  ALU.mult).then_inc(att_out, 1)

            for n in range(n0, n1 + 3):
                if n < n1:
                    mask(n)
                if n0 == 0 and 2 <= n < n1 + 2:
                    copy_b(n - 2)
                if n >= n0 + 3:
                    out(n - 3)
                if n < 56 and n % NT == 2:
                    stack_low(n // NT + 1)
                if meanwhile:
                    meanwhile(n - n0)

        def bias1(n):
            i, h, _ = UNITS[n]
            if i == 0:
                dve.wait_ge(bias_loaded[h % 2], 16 * (h // 2 + 1))
            return BIAS[h % 2][:, 896 - i * P:896 - i * P + S]

        attention(0, 64, bias1)

        def turned_lo(n, base, xbase):
            for k in range(n):
                dve.wait_ge(turned, base + k + 1)
                dve.wait_ge(x_hi, xbase + k + 1)
                dve.tensor_tensor(XL[:, k, :], TPf[(base + k) % 2], XH[:, k, :].bitcast(F32),
                                  ALU.subtract).then_inc(x_split, 1)

        turned_lo(8, 12, 8)

        for m in range(8):
            g = OUT1 + m
            lo(g + 1, (g + 1) % 2)
            dve.wait_ge(slab_done, g + 2)
            dve.tensor_copy(ACC[:, m, :], Gf[g % 2]).then_inc(psum_free[g % 2], 1)
            if m:
                add_square(m - 1)
        norm(D, RMS_EPS, first=7)
        lo(FFN1 + 1, (FFN1 + 1) % 2)

        def low_scaled(k):
            dve.wait_ge(x_hi, 16 + k + 1)
            dve.scalar_tensor_tensor(out=XL[:, k, :], in0=XT[:, k, :], scalar=V("g_pre_ffn", k),
                                     in1=XH[:, k, :].bitcast(F32), op0=ALU.mult, op1=ALU.subtract).then_inc(x_split, 1)

        residual(ACC, lambda k: V("g_post_mix", k), 0, low_scaled)
        norm(D, RMS_EPS)
        seq(dve.tensor_copy(RBS[:, :], TPf[0]))

        def ffn(g0, which, scale):
            def group(grp, first=False, last=False):
                for m in range(16):
                    g, b = g0 + m, (g0 + m) % 2
                    if not (first and m == 0):
                        lo(grp * 16 + (g + 1), 1 - b)
                    if which == 0 and (m < 8 or m % 2):
                        a = m if m < 8 else 8 + (m - 8) // 2
                        dve.wait_ge(ada_prod, grp * 12 + (a + 1))
                        dve.wait_ge(mod_col, grp * 12 + (a + 1))
                        dve.tensor_reduce(RED[a % 2][:, :], ADA[a % 2][:, :, :].rearrange("p k n -> p n k"), AX.X,
                                          ALU.add).then_inc(ada_red, 1)
                    if m < 8:
                        u = grp * 8 + (32 * which + m)
                        if which == 0:
                            dve.wait_ge(slab_done, grp * 16 + (g + 2))
                            dve.wait_ge(usq_ready, u + 1)
                            if m:
                                dve.wait_ge(u_split, u)
                            dve.scalar_tensor_tensor(out=RELU[:, :], in0=Gf[b], scalar=0.0, in1=RBS[:, :], op0=ALU.max,
                                                     op1=ALU.mult).then_inc(psum_free[b], 1)
                        else:
                            dve.wait_ge(psum_free[b], grp * 8 + (g // 2 + 2))
                            if m:
                                dve.wait_ge(u_split, u)
                            dve.tensor_tensor(USQ[:, :], RELU[:, :], RELU[:, :], ALU.mult).then_inc(usq_ready, 1)
                        dve.wait_ge(usq_ready, u + 2)
                        dve.wait_ge(u_hi, u + 1)
                        dve.tensor_tensor(UL[:, m, :], (USQ if which else RELU)[:, :], UH[:, m, :].bitcast(F32),
                                          ALU.subtract).then_inc(u_split, 1)
                    else:
                        dve.wait_ge(slab_done, grp * 16 + (g + 2))
                        if first:
                            if m == 8:
                                dve.wait_ge(spilled, 16)
                            ins = dve.tensor_copy(XT[:, m - 8, :], Gf[b])
                        else:
                            ins = dve.scalar_tensor_tensor(out=XT[:, m - 8, :], in0=Gf[b], scalar=scale(m - 8),
                                                           in1=XT[:, m - 8, :], op0=ALU.mult, op1=ALU.add)
                        ins.then_inc(psum_free[b], 1)
                        if last and m > 8:
                            add_square(m - 9, SQF, SSQF)

            if which == 0:
                group(0, first=True)
            with dve.Fori(1 - which, GROUPS - 1) as grp:
                group(grp)
            group(GROUPS - 1, last=True)

        ffn(FFN1, 0, lambda k: 1.0)
        dve.wait_ge(mod_col, 50)
        seq(dve.tensor_tensor(mod[:, :], TP[1][:, 1, 0:48], vec[:, VCOL["b_ada"]:VCOL["b_ada"] + 48], ALU.add))
        for r, name in enumerate(("g_mix", "g_mlp")):
            last = dve.scalar_tensor_tensor(out=scl[:, 8 * r:8 * r + 8], in0=mod[:, 24 * r + 8:24 * r + 16], scalar=1.0,
                                            in1=vec[:, VCOL[name]:VCOL[name] + 8], op0=ALU.add, op1=ALU.mult)
        last.then_inc(mod_ready, 1)
        norm(D, RMS_EPS, KT_N, SQF, SSQF, DGF, first=7)
        residual(XT, lambda k: V("g_post_ffn", k), 2)
        norm(D, RMS_EPS)
        dve.wait_ge(mod_ready, 1)
        split_norm(lambda k: scl[:, k:k + 1], lambda k: mod[:, k:k + 1], 24)

        lo(IN2 + 1, (IN2 + 1) % 2)
        dve.wait_ge(pos_loaded, 16)
        seq(dve.tensor_scalar(T1[:, :], POSI[:, :], freq, None, ALU.mult))
        MAGIC = 1.5 * 2.0 ** 23
        C1 = 6.28125
        C2 = float(np.float32(round((2 * np.pi - C1) * 2 ** 21) / 2 ** 21))
        C3 = float(2 * np.pi - C1 - C2)
        for tab, quarter in ((COS, 0.25), (SIN, 0.0)):
            seq(dve.tensor_scalar(TK2[:, :], T1[:, :], float(1 / (2 * np.pi)), quarter, ALU.mult, ALU.add))
            seq(dve.tensor_scalar(TK2[:, :], TK2[:, :], MAGIC, MAGIC, ALU.add, ALU.subtract))
            src = T1
            for c in (C1, C2, C3):
                seq(dve.scalar_tensor_tensor(out=tab[:, :], in0=TK2[:, :], scalar=-c, in1=src[:, :], op0=ALU.mult,
                                             op1=ALU.add))
                src = tab
            seq(dve.tensor_scalar(tab[:, :], tab[:, :], float(2 * np.pi * quarter), 3.1415925, ALU.add, ALU.min))
            dve.tensor_scalar(tab[:, :], tab[:, :], -3.1415925, None, ALU.max).then_inc(angle_ready, 1)

        def rope(m, dst):
            if m == 0:
                dve.wait_ge(rope_ready, 2)
            dve.wait_ge(swapped, m + 1)
            dve.tensor_tensor(T1[:, :], T2[m % 2][:, :], COS[:, :], ALU.mult)
            seq(dve.tensor_tensor(dst, TPf[0], SIN[:, :], ALU.mult))
            dve.tensor_tensor(dst, dst, T1[:, :], ALU.add).then_inc(roped, 1)

        for m in range(1, 5):
            lo(IN2 + m + 1, (IN2 + m + 1) % 2)
            rope(m - 1, KI[:, :] if m == 1 else QI[:, m - 2, :])
            if m == 1:
                dve.wait_ge(wi_turned, 1)
                seq(dve.tensor_scalar(wi[:, :], TP[1][:, 0, 0:8 * NT], float(np.float32(HEADS ** -0.5)), None, ALU.mult))
        rope(4, QI[:, 3, :])
        n = 0
        for i in range(TOPK_TILE, NT):
            sc = SC[:, score_at(i):score_at(i + 1)]
            for h in range(HEADS):
                w = wi[:, 8 * i + h:8 * i + h + 1]
                dve.wait_ge(idx_relu, n + 1)
                r = T2[n % 2][:, 0:P * (i + 1)]
                if h == 0:
                    dve.tensor_scalar(sc, r, w, None, ALU.mult).then_inc(idx_added, 1)
                else:
                    dve.wait_ge(idx_added, n)
                    dve.scalar_tensor_tensor(out=sc, in0=r, scalar=w, in1=sc, op0=ALU.mult, op1=ALU.add).then_inc(idx_added, 1)
                n += 1

        tiles = [(n, i, SC[:, score_at(i):score_at(i + 1)]) for n, i in enumerate(range(TOPK_TILE, NT))]

        t_bit, t_counted = Tally(cand_ready), Tally(act_counted)

        def count(which, op, level):
            for r, n in enumerate(which):
                if r >= 2:
                    dve.wait_ge(dve_seq, d.n - 1)
                _, i, sc = tiles[n]
                d.inc(dve.tensor_scalar(JUNK[:, r % 2, 0:P * (i + 1)], sc, level(n), None, op, ALU.add,
                                        accum_out=cnt[:, n:n + 1]))
            d.wait(dve)

        def select_sign():
            dve.wait_ge(idx_masked, NQ)
            count(range(NQ), ALU.is_ge, lambda n: 0.0)
            seq(dve.tensor_scalar(sgn[:, :], cnt[:, :], float(TOPK), None, ALU.is_ge))
            for n, i, sc in tiles:
                below = P * (i + 1) - TOPK + 1
                last = dve.tensor_scalar(need[:, n:n + 1], sgn[:, n:n + 1], float(TOPK - below), float(below),
                                         ALU.mult, ALU.add)
            seq(last)
            for n, i, sc in tiles:
                k = 2 if n in ACT_TILES else 1
                dve.tensor_scalar(most[:, n:n + 1], need[:, n:n + 1], -float(k), float(P * (i + 1) + k - 1),
                                  ALU.mult, ALU.add)
            dve.memset(mag[:, :], 0)
            seq(dve.tensor_scalar(sgn[:, :], sgn[:, :], 2.0, -1.0, ALU.mult, ALU.add))
            for n, i, sc in tiles:
                last = dve.tensor_scalar(sc, sc, sgn[:, n:n + 1], None, ALU.mult)
            seq(last)

        def select_bit(bit):
            t_bit.inc(dve.tensor_scalar(cand[:, :], mag[:, :], 1 << bit, None, ALU.bitwise_or))
            t_bit.wait(dve)
            count(DVE_TILES, ALU.is_lt, lambda n: cand[:, n:n + 1].bitcast(F32))
            t_counted.wait(dve, len(ACT_TILES))
            seq(dve.tensor_tensor(keep[:, :], cnt[:, :], most[:, :], ALU.is_le))
            seq(dve.copy_predicated(mag[:, :], keep[:, :], cand[:, :]))

        def select_next():
            half_ulp = 2.0 ** -24 * (1 + 2.0 ** -23)
            magf = mag[:, :].bitcast(F32)
            seq(dve.scalar_tensor_tensor(out=above_mag[:, :], in0=magf, scalar=half_ulp, in1=magf, op0=ALU.mult,
                                         op1=ALU.add))
            count(ACT_TILES, ALU.is_ge, lambda n: above_mag[:, n:n + 1])
            for n in ACT_TILES:
                seq(dve.tensor_tensor(keep[:, n:n + 1], cnt[:, n:n + 1], need[:, n:n + 1], ALU.is_ge))
                seq(dve.copy_predicated(mag[:, n:n + 1], keep[:, n:n + 1], above_mag[:, n:n + 1].bitcast(U32)))

        def select_masks():
            seq(dve.tensor_tensor(thr[:, :], mag[:, :].bitcast(F32), sgn[:, :], ALU.mult))
            for n, i, sc in tiles:
                w = P * (i + 1)
                above, equal, rank = TK1[:, 0:w], TK2[:, 0:w], T1[:, 0:w]
                seq(dve.tensor_scalar(sc, sc, sgn[:, n:n + 1], None, ALU.mult))
                dve.tensor_scalar(equal, sc, thr[:, n:n + 1], None, ALU.is_equal)
                seq(dve.tensor_scalar(above, sc, thr[:, n:n + 1], None, ALU.is_gt, ALU.add, accum_out=cnt[:, n:n + 1]))
                seq(dve.tensor_scalar(need[:, n:n + 1], cnt[:, n:n + 1], -1.0, float(TOPK), ALU.mult, ALU.add))
                seq(dve.tensor_tensor_scan(rank, equal, equal, 0.0, ALU.add, ALU.max))
                seq(dve.scalar_tensor_tensor(out=equal, in0=rank, scalar=need[:, n:n + 1], in1=equal, op0=ALU.is_le,
                                             op1=ALU.mult))
                seq(dve.scalar_tensor_tensor(out=sc, in0=equal, scalar=-1.0, in1=above, op0=ALU.add, op1=ALU.add))
                seq(dve.tensor_scalar(sc, sc, FAR, None, ALU.mult))

        bits = list(range(BITS - 1, -1, -1))
        select_sign()
        for m in range(5, 19):
            lo(IN2 + m + 1, (IN2 + m + 1) % 2)
            if 6 <= m <= 10:
                rope(m - 1, QT2[:, m - 6, :] if m < 10 else KT2[:, :])
            if m == 11:
                dve.wait_ge(v2_turned, 1)
                dve.tensor_copy(V2[:, :, :].rearrange("p t c -> p (t c)"), TPf[1]).then_inc(v2_ready, 1)
            if m >= 13 and m % 2 == 1:
                j = (m - 13) // 2
                g = IN2 + m - 1
                dve.wait_ge(psum_free[g % 2], g // 2 + 2)
                dve.tensor_tensor(CU[:, j, PAD:PAD + S], CU[:, j, PAD:PAD + S], SIG[:, :], ALU.mult).then_inc(glu_ready, 1)
            for _ in range(bits_beside.get(m, 0)):
                select_bit(bits.pop(0))
            if m == 17:
                select_next()
        g = IN2 + 18
        dve.wait_ge(psum_free[g % 2], g // 2 + 2)
        dve.tensor_tensor(CU[:, 3, PAD:PAD + S], CU[:, 3, PAD:PAD + S], SIG[:, :], ALU.mult).then_inc(glu_ready, 1)
        select_masks()

        def key_low(r):
            own = halves(r)[0]
            dve.wait_ge(stack_hi, STACKED_HI + 2 * r + 1)
            dve.tensor_tensor(KL2[own, :], KT2[own, :], KS2[r][own, :].bitcast(F32), ALU.subtract).then_inc(stack_lo, 1)

        def query_low(h):
            own, other = halves(h // 4)
            dve.wait_ge(stack_hi, STACKED_HI + 4 + h + 1)
            dve.tensor_tensor(QS2[h][other, :], QT2[own, h % 4, :], QS2[h][own, :].bitcast(F32),
                              ALU.subtract).then_inc(stack_lo, 1)

        for r in range(2):
            key_low(r)
        for h in range(2):
            query_low(h)

        dve.wait_ge(glu_ready, 4)
        dve.wait_ge(pool_seq, 2)
        conv0 = d.n
        taps = [(tap, j) for tap in range(CONV_K) for j in range(4)]
        done = {}

        per_unit = [[2, 2, 2, 3, 4, 5, 6, 7][UNITS[n][0]] for n in range(64, 128)]
        until = [0]
        for twice in per_unit:
            until.append(until[-1] + twice)
        assert until[-1] >= 2 * len(taps)

        def conv(step):
            if step + 2 < HEADS:
                query_low(step + 2)
            if step >= len(per_unit):
                return
            for tap, j in taps[until[step] // 2:until[step + 1] // 2]:
                w = V("conv_w", j * CONV_K + tap)
                src = CU[:, j, tap:tap + S]
                if tap == 0:
                    ins = dve.tensor_scalar(YC[:, j, :], src, w, V("conv_b", j), ALU.mult, ALU.add)
                else:
                    dve.wait_ge(dve_seq, done[j])
                    ins = dve.scalar_tensor_tensor(out=YC[:, j, :], in0=src, scalar=w, in1=YC[:, j, :], op0=ALU.mult,
                                                   op1=ALU.add)
                if tap == CONV_K - 1:
                    ins.then_inc(conv_ready, 1)
                else:
                    d.inc(ins)
                    done[j] = d.n

        def bias2(n):
            i = UNITS[n][0]
            if i >= TOPK_TILE:
                return SC[:, score_at(i):score_at(i + 1)]
            if n == 64:
                dve.wait_ge(mask01, 2)
            return MASK01[:, 0:P] if i == 0 else MASK01[:, P:3 * P]

        attention(64, 128, bias2, conv)
        turned_lo(4, 20, 32)
        dve.wait_ge(conv_mean, 1)
        for j in range(4):
            dve.scalar_tensor_tensor(out=YC[:, j, :], in0=TPf[1], scalar=-1.0 / ATT, in1=YC[:, j, :], op0=ALU.mult,
                                     op1=ALU.add).then_inc(conv_centred, 1)
        norm(ATT, RMS_EPS, 4, SQ2, SSQ2, DG2)
        for j in range(4):
            t_hf.inc(dve.tensor_tensor(YC[:, j, :], YC[:, j, :], TPf[0], ALU.mult))
        for j in range(4):
            dve.wait_ge(x_hi, 36 + j + 1)
            dve.tensor_tensor(XL[:, 4 + j, :], HC[j % 2][:, :], XH[:, 4 + j, :].bitcast(F32), ALU.subtract).then_inc(x_split, 1)

        dve.wait_ge(x_back, 16)
        for m in range(8):
            g = OUT2 + m
            lo(g + 1, (g + 1) % 2)
            dve.wait_ge(slab_done, g + 2)
            dve.scalar_tensor_tensor(out=XT[:, m, :], in0=Gf[g % 2], scalar=mod[:, 16 + m:17 + m], in1=XT[:, m, :],
                                     op0=ALU.mult, op1=ALU.add).then_inc(psum_free[g % 2], 1)
            if m:
                add_square(m - 1)
        norm(D, RMS_EPS, first=7)
        split_norm(lambda k: scl[:, 8 + k:9 + k], lambda k: mod[:, 24 + k:25 + k], 40)
        ffn(FFN2, 1, lambda k: mod[:, 40 + k:41 + k])
        norm(D, RMS_EPS, KT_N, SQF, SSQF, DGF, first=7)
        for k in range(KT_N):
            t_hf.inc(dve.scalar_tensor_tensor(out=XT[:, k, :], in0=XT[:, k, :], scalar=V("g_final", k), in1=TPf[0],
                                              op0=ALU.mult, op1=ALU.mult))

    return ctx


def in_slabs(w, cols=None):
    if cols is not None:
        w = np.concatenate([w[:, c:c + n] for c, n in cols], axis=1)
    m = w.shape[1] // P
    return w.reshape(KT_N, P, m, P).transpose(2, 1, 0, 3).reshape(m, P, S)


def columns(v):
    return np.asarray(v).reshape(-1, P).T


def kernel(**inputs):
    import concourse.bacc as bacc
    from concourse.bass_utils import run_bass_kernel_spmd

    a = {k: np.asarray(v) for k, v in inputs.items()}
    w_in2 = a["w_in_2"][0]
    one, pair = P, DH
    heads = [(h * DH + 4 * DH * r, pair) for h in range(4) for r in range(2)]
    in2 = ([(1280, one)] + [(768 + one * m, one) for m in range(4)] + heads + [(512, one), (640, one)]
           + [(1352 + ATT * r + one * j, one) for j in range(4) for r in range(2)])

    def feed_forward(w1, w2):
        parts = []
        for g in range(GROUPS):
            parts += [in_slabs(w1[:, g * D:(g + 1) * D]), in_slabs(w2[g * D:(g + 1) * D, :])]
        return parts

    w_in1 = a["w_in"][0]
    slabs = np.concatenate(
        [in_slabs(w_in1, ((3 * ATT, 2 * ATT), (0, 3 * ATT))), in_slabs(a["w_out"][0])] + feed_forward(a["w_ff1"][0], a["w_ff2"][0])
        + [in_slabs(w_in2, in2), in_slabs(a["w_out_2"][0])] + feed_forward(a["w_up_2"][0], a["w_down_2"][0])
        + [in_slabs(w_in1[:, 0:P])])
    packed = {
        "g_pre_mix": columns(a["g_pre_mix"]), "g_post_mix": columns(a["g_post_mix"]),
        "g_pre_ffn": columns(a["g_pre_ffn"]), "g_post_ffn": columns(a["g_post_ffn"]), "sgu_b": a["sgu_b"][0].T,
        "b_ada": columns(a["b_ada_2"]), "g_mix": columns(a["g_mix_2"]),
        "conv_w": a["conv_w_2"][0].reshape(CONV_K, 4, P).transpose(2, 1, 0).reshape(P, 4 * CONV_K),
        "conv_b": columns(a["conv_b_2"]), "conv_g": columns(a["conv_norm_g_2"]), "conv_nb": columns(a["conv_norm_b_2"]),
        "g_mlp": columns(a["g_mlp_2"]), "g_final": columns(a["g_final_2"]), "c": columns(a["c_2"]),
    }
    consts = np.zeros((P, N_CONST), np.float32)
    consts[:, 0:P] = np.eye(P)
    for base in range(0, P, DH):
        for r in range(8):
            consts[base + 8 + r, P + base + r] = -1.0
            consts[base + r, P + base + 8 + r] = 1.0
            f = np.power(np.float32(500000.0), np.float32(-r * 2.0 / 16))
            consts[base + r, 4 * P] = consts[base + 8 + r, 4 * P] = f
    consts[:, 2 * P:3 * P] = 1.0
    consts[:, 3 * P:4 * P] = np.eye(P)[::-1]
    arrays = {
        "slabs": slabs, "ada": in_slabs(a["w_ada_2"][0]), "xT": a["x"][0].T,
        "vecs": np.concatenate([packed[name] for name, _ in VECS], axis=1),
        "lnrow": np.concatenate([a["sgu_ln_g"], a["sgu_ln_b"]]),
        "sgu_wT": a["sgu_w"][0].transpose(2, 0, 1).reshape(P, SGU_G * P),
        "rel_bias": a["rel_bias"], "positions": a["positions_2"], "consts": consts, "hot": t5_tables(),
    }
    nc = bacc.Bacc("TRN2", target_bir_lowering=False, num_devices=1)
    args = []
    for name in arrays:
        arrays[name] = np.ascontiguousarray(arrays[name])
        args.append(nc.dram_tensor(name, arrays[name].shape, mybir.dt.from_np(arrays[name].dtype), kind="ExternalInput").ap())
    args.append(nc.dram_tensor("outT", (D, S), F32, kind="ExternalOutput").ap())
    with build(nc, *args):
        pass
    r = run_bass_kernel_spmd(nc, [arrays], core_ids=[0])
    return np.ascontiguousarray(r.results[0]["outT"].T).reshape(1, S, D)
```
